# Optimizing a Trainium2 kernel written in Bass

```python
import jax
import jax.numpy as jnp
from jax import lax
import numpy as np

D_MODEL = 1024
BATCH = 1
SEQ = 256
DEPTH = 2

CTX_LEN = 256
GRID_W = 64
N_MOD = 9
NORM_EPS = 1e-6
D_FF = 2816
ATTN_HEADS = 8
ATTN_KV_HEADS = 2
ATTN_GROUP = ATTN_HEADS // ATTN_KV_HEADS
ATTN_HEAD_DIM = 128
WINDOW = 128
ATTN_BLOCK = 128
ROPE_THETA = 10000.0
GLA_HEADS = 4
GLA_KEY_DIM = 128
GLA_VALUE_DIM = 256
GLA_GATE_RANK = 16
GLA_GATE_TEMP = 16.0
GLA_CHUNK = 64
ATTN_Q_W = ATTN_HEADS * ATTN_HEAD_DIM
ATTN_KV_W = ATTN_KV_HEADS * ATTN_HEAD_DIM
GLA_K_W = GLA_HEADS * GLA_KEY_DIM
GLA_V_W = GLA_HEADS * GLA_VALUE_DIM
CTX_SIDE_COLS = (ATTN_KV_W, ATTN_KV_W, GLA_K_W, GLA_V_W, GLA_GATE_RANK, GLA_GATE_RANK)
QUERY_SIDE_COLS = (ATTN_Q_W, GLA_K_W, GLA_V_W, D_MODEL, D_MODEL)
N_CTX_SIDE = sum(CTX_SIDE_COLS)
IN_COLS = N_CTX_SIDE + sum(QUERY_SIDE_COLS)

kernel_name = 'hybrid_flow_backbone_block'

def split_cols(z, sizes):
    idx = [int(i) for i in np.cumsum(sizes)[:-1]]
    return jnp.split(z, idx, axis=-1)

def flip_time(t):
    return jnp.flip(t, axis=1)

def rmsnorm(x, w):
    x32 = x.astype(jnp.float32)
    y = x32 * lax.rsqrt(jnp.mean(x32 * x32, axis=-1, keepdims=True) + NORM_EPS)
    return (y * w.astype(jnp.float32)).astype(x.dtype)

def adaln(cond, w, b):
    m = (cond @ w + b)[..., None, :]
    return jnp.split(m, N_MOD, axis=-1)

def modulate(h, shift, scale):
    return h * (1 + scale) + shift

def swiglu(h, w13, w2):
    up, gate = jnp.split(h @ w13, 2, axis=-1)
    return (jax.nn.silu(gate) * up) @ w2

def axial_rope_tables(n_tokens):
    rows = n_tokens // GRID_W
    row = jnp.repeat(jnp.arange(rows), GRID_W).astype(jnp.float32)
    col = jnp.tile(jnp.arange(GRID_W), rows).astype(jnp.float32)
    half = ATTN_HEAD_DIM // 2
    inv_freq = ROPE_THETA ** (-jnp.arange(0, half, 2, dtype=jnp.float32) / half)
    ang_r = row[:, None] * inv_freq[None, :]
    ang_c = col[:, None] * inv_freq[None, :]
    return (jnp.cos(ang_r), jnp.sin(ang_r), jnp.cos(ang_c), jnp.sin(ang_c))

def rotate_pairs(x, cos, sin):
    x1, x2 = jnp.split(x.astype(jnp.float32), 2, axis=-1)
    cos = cos[:, None, :]
    sin = sin[:, None, :]
    return jnp.concatenate([x1 * cos - x2 * sin, x1 * sin + x2 * cos], axis=-1)

def axial_rope(x, tabs):
    cos_r, sin_r, cos_c, sin_c = tabs
    x_row, x_col = jnp.split(x, 2, axis=-1)
    return jnp.concatenate([rotate_pairs(x_row, cos_r, sin_r), rotate_pairs(x_col, cos_c, sin_c)], axis=-1).astype(x.dtype)

def window_attention(q, k, v, kc, vc, sink):
    B, S = q.shape[:2]
    L = kc.shape[1]
    nb = S // ATTN_BLOCK
    scale = ATTN_HEAD_DIM ** -0.5
    qb = q.reshape(B, nb, ATTN_BLOCK, ATTN_KV_HEADS, ATTN_GROUP, ATTN_HEAD_DIM)

    def band(t):
        tp = jnp.pad(t, ((0, 0), (ATTN_BLOCK, ATTN_BLOCK), (0, 0), (0, 0)))
        tp = tp.reshape(B, nb + 2, ATTN_BLOCK, ATTN_KV_HEADS, ATTN_HEAD_DIM)
        return jnp.concatenate([tp[:, :-2], tp[:, 1:-1], tp[:, 2:]], axis=2)

    kw, vw = band(k), band(v)
    qi = jnp.arange(ATTN_BLOCK)[:, None]
    kj = jnp.arange(3 * ATTN_BLOCK)[None, :] - ATTN_BLOCK
    key_pos = jnp.arange(nb)[:, None, None] * ATTN_BLOCK + kj[None]
    mask = (jnp.abs(kj - qi) <= WINDOW)[None] & (key_pos >= 0) & (key_pos < S)
    s_win = jnp.einsum('bnqhgd,bnkhd->bnhgqk', qb, kw).astype(jnp.float32) * scale
    s_win = jnp.where(mask[None, :, None, None], s_win, -jnp.inf)
    s_ctx = jnp.einsum('bnqhgd,blhd->bnhgql', qb, kc).astype(jnp.float32) * scale
    s_sink = jnp.broadcast_to(sink.reshape(ATTN_KV_HEADS, ATTN_GROUP, 1, 1).astype(jnp.float32), s_ctx.shape[:-1] + (1,))
    p = jax.nn.softmax(jnp.concatenate([s_win, s_ctx, s_sink], axis=-1), axis=-1).astype(v.dtype)
    p_win = p[..., :3 * ATTN_BLOCK]
    p_ctx = p[..., 3 * ATTN_BLOCK:3 * ATTN_BLOCK + L]
    o = jnp.einsum('bnhgqk,bnkhd->bnqhgd', p_win, vw) + jnp.einsum('bnhgql,blhd->bnqhgd', p_ctx, vc)
    return o.reshape(B, S, ATTN_Q_W)

def context_attention(qc, kc, vc, sink):
    B, L = qc.shape[:2]
    scale = ATTN_HEAD_DIM ** -0.5
    qg = qc.reshape(B, L, ATTN_KV_HEADS, ATTN_GROUP, ATTN_HEAD_DIM)
    s = jnp.einsum('blhgd,bmhd->bhglm', qg, kc).astype(jnp.float32) * scale
    s_sink = jnp.broadcast_to(sink.reshape(ATTN_KV_HEADS, ATTN_GROUP, 1, 1).astype(jnp.float32), s.shape[:-1] + (1,))
    p = jax.nn.softmax(jnp.concatenate([s, s_sink], axis=-1), axis=-1).astype(vc.dtype)
    o = jnp.einsum('bhglm,bmhd->blhgd', p[..., :L], vc)
    return o.reshape(B, L, ATTN_Q_W)

def gla_log_decay(lowrank, w, b):
    B, T = lowrank.shape[:2]
    logit = (lowrank @ w + b).astype(jnp.float32)
    return (jax.nn.log_sigmoid(logit) / GLA_GATE_TEMP).reshape(B, T, GLA_HEADS, GLA_KEY_DIM)

def gla_chunk_scan(q, k, v, g, s0):
    B, T, H, dk = q.shape
    dv = v.shape[-1]
    nc = T // GLA_CHUNK
    out_dtype = v.dtype

    def chunks(t):
        return jnp.moveaxis(t.astype(jnp.float32).reshape(B, nc, GLA_CHUNK, H, t.shape[-1]), 1, 0)

    causal = jnp.tril(jnp.ones((GLA_CHUNK, GLA_CHUNK), dtype=bool))

    def step(s, inp):
        qc, kc, vc, gc = inp
        b = jnp.cumsum(gc, axis=1)
        o_inter = jnp.einsum('bchd,bhde->bche', qc * jnp.exp(b), s)
        diff = b[:, :, None] - b[:, None, :]
        decay = jnp.exp(jnp.where(causal[None, :, :, None, None], diff, -jnp.inf))
        a = jnp.einsum('bijhd,bjhd->bhij', qc[:, :, None] * decay, kc)
        o_intra = jnp.einsum('bhij,bjhe->bihe', a, vc)
        b_last = b[:, -1]
        s_new = jnp.exp(b_last)[..., None] * s + jnp.einsum('bchd,bche->bhde', kc * jnp.exp(b_last[:, None] - b), vc)
        return s_new, o_inter + o_intra

    s_final, o = lax.scan(step, s0.astype(jnp.float32), (chunks(q), chunks(k), chunks(v), chunks(g)))
    o = jnp.moveaxis(o, 0, 1).reshape(B, T, H, dv).astype(out_dtype)
    return o, s_final

def gla_final_state(k, v, g):
    k = k.astype(jnp.float32)
    v = v.astype(jnp.float32)
    b = jnp.cumsum(g.astype(jnp.float32), axis=1)
    w = jnp.exp(b[:, -1:] - b)
    return jnp.einsum('bthd,bthe->bhde', k * w, v)

def gla_output(o, r, w):
    B, T = r.shape[:2]
    return rmsnorm(o, w).reshape(B, T, GLA_V_W) * jax.nn.silu(r)

def merge_branches(y_attn, y_gla, gate_a, gate_g, w_ba, w_bg, w_out):
    return (jax.nn.sigmoid(gate_a) * (y_attn @ w_ba) + jax.nn.sigmoid(gate_g) * (y_gla @ w_bg)) @ w_out

def mixer(h, hc, w_in, q_norm_w, k_norm_w, sink, gw_f, gb_f, gw_b, gb_b, gla_norm_w, w_ba, w_bg, w_out, tabs, need_ctx_out):
    B, S, _ = h.shape
    L = hc.shape[1]
    ak, av, gk, gv, glr_f, glr_b, aq, gq, gr, gate_a, gate_g = split_cols(h @ w_in, CTX_SIDE_COLS + QUERY_SIDE_COLS)
    akc, avc, gkc, gvc, glrc_f, glrc_b = split_cols(hc @ w_in[:, :N_CTX_SIDE], CTX_SIDE_COLS)

    q = axial_rope(rmsnorm(aq.reshape(B, S, ATTN_HEADS, ATTN_HEAD_DIM), q_norm_w), tabs)
    k = axial_rope(rmsnorm(ak.reshape(B, S, ATTN_KV_HEADS, ATTN_HEAD_DIM), k_norm_w), tabs)
    v = av.reshape(B, S, ATTN_KV_HEADS, ATTN_HEAD_DIM)
    kc = rmsnorm(akc.reshape(B, L, ATTN_KV_HEADS, ATTN_HEAD_DIM), k_norm_w)
    vc = avc.reshape(B, L, ATTN_KV_HEADS, ATTN_HEAD_DIM)
    y_attn = window_attention(q, k, v, kc, vc, sink)

    gla_scale = GLA_KEY_DIM ** -0.5
    qg = gq.reshape(B, S, GLA_HEADS, GLA_KEY_DIM) * gla_scale
    kg = gk.reshape(B, S, GLA_HEADS, GLA_KEY_DIM)
    vg = gv.reshape(B, S, GLA_HEADS, GLA_VALUE_DIM)
    g_f = gla_log_decay(glr_f, gw_f, gb_f)
    g_b = gla_log_decay(glr_b, gw_b, gb_b)
    kgc = gkc.reshape(B, L, GLA_HEADS, GLA_KEY_DIM)
    vgc = gvc.reshape(B, L, GLA_HEADS, GLA_VALUE_DIM)
    gc_f = gla_log_decay(glrc_f, gw_f, gb_f)
    gc_b = gla_log_decay(glrc_b, gw_b, gb_b)

    if need_ctx_out:
        aqc, gqc, grc, gate_ac, gate_gc = split_cols(hc @ w_in[:, N_CTX_SIDE:], QUERY_SIDE_COLS)
        qc = rmsnorm(aqc.reshape(B, L, ATTN_HEADS, ATTN_HEAD_DIM), q_norm_w)
        yc_attn = context_attention(qc, kc, vc, sink)
        qgc = gqc.reshape(B, L, GLA_HEADS, GLA_KEY_DIM) * gla_scale
        zero = jnp.zeros((B, GLA_HEADS, GLA_KEY_DIM, GLA_VALUE_DIM), jnp.float32)
        oc_f, s_f = gla_chunk_scan(qgc, kgc, vgc, gc_f, zero)
        oc_b, s_b = gla_chunk_scan(flip_time(qgc), flip_time(kgc), flip_time(vgc), flip_time(gc_b), zero)
        yc_gla = gla_output(oc_f + flip_time(oc_b), grc, gla_norm_w)
        yc = merge_branches(yc_attn, yc_gla, gate_ac, gate_gc, w_ba, w_bg, w_out)
    else:
        s_f = gla_final_state(kgc, vgc, gc_f)
        s_b = gla_final_state(flip_time(kgc), flip_time(vgc), flip_time(gc_b))
        yc = None

    o_f, _ = gla_chunk_scan(qg, kg, vg, g_f, s_f)
    o_b, _ = gla_chunk_scan(flip_time(qg), flip_time(kg), flip_time(vg), flip_time(g_b), s_b)
    y_gla = gla_output(o_f + flip_time(o_b), gr, gla_norm_w)
    y = merge_branches(y_attn, y_gla, gate_a, gate_g, w_ba, w_bg, w_out)
    return y, yc

def setup_inputs(seed: int = 0) -> dict:
    key = jax.random.key(seed)
    ks = jax.random.split(key, 24)
    f32 = jnp.float32

    def nrm(k, shape, scale):
        return jax.random.normal(k, shape, f32) * scale

    return {
        'x': nrm(ks[0], (BATCH, SEQ, D_MODEL), 1.0),
        'c': nrm(ks[1], (BATCH, D_MODEL), 1.0),
        'ctx': nrm(ks[2], (BATCH, CTX_LEN, D_MODEL), 1.0),
        'c_ctx': nrm(ks[3], (D_MODEL,), 1.0),
        'w_mod': nrm(ks[4], (DEPTH, D_MODEL, N_MOD * D_MODEL), 0.5 * D_MODEL ** -0.5),
        'b_mod': nrm(ks[5], (DEPTH, N_MOD * D_MODEL), 0.02),
        'norm_w': 1.0 + nrm(ks[6], (DEPTH, 3, D_MODEL), 0.02),
        'ffn1_w13': nrm(ks[7], (DEPTH, D_MODEL, 2 * D_FF), D_MODEL ** -0.5),
        'ffn1_w2': nrm(ks[8], (DEPTH, D_FF, D_MODEL), D_FF ** -0.5),
        'ffn2_w13': nrm(ks[9], (DEPTH, D_MODEL, 2 * D_FF), D_MODEL ** -0.5),
        'ffn2_w2': nrm(ks[10], (DEPTH, D_FF, D_MODEL), D_FF ** -0.5),
        'w_in': nrm(ks[11], (DEPTH, D_MODEL, IN_COLS), D_MODEL ** -0.5),
        'q_norm_w': 1.0 + nrm(ks[12], (DEPTH, ATTN_HEAD_DIM), 0.02),
        'k_norm_w': 1.0 + nrm(ks[13], (DEPTH, ATTN_HEAD_DIM), 0.02),
        'attn_sink': nrm(ks[14], (DEPTH, ATTN_HEADS), 0.5),
        'gla_gate_w_fwd': nrm(ks[15], (DEPTH, GLA_GATE_RANK, GLA_K_W), GLA_GATE_RANK ** -0.5),
        'gla_gate_b_fwd': nrm(ks[16], (DEPTH, GLA_K_W), 0.1),
        'gla_gate_w_bwd': nrm(ks[17], (DEPTH, GLA_GATE_RANK, GLA_K_W), GLA_GATE_RANK ** -0.5),
        'gla_gate_b_bwd': nrm(ks[18], (DEPTH, GLA_K_W), 0.1),
        'gla_norm_w': 1.0 + nrm(ks[19], (DEPTH, GLA_VALUE_DIM), 0.02),
        'w_branch_attn': nrm(ks[20], (DEPTH, ATTN_Q_W, D_MODEL), ATTN_Q_W ** -0.5),
        'w_branch_gla': nrm(ks[21], (DEPTH, GLA_V_W, D_MODEL), GLA_V_W ** -0.5),
        'w_out': nrm(ks[22], (DEPTH, D_MODEL, D_MODEL), D_MODEL ** -0.5),
    }

def reference(x, c, ctx, c_ctx, w_mod, b_mod, norm_w, ffn1_w13, ffn1_w2, ffn2_w13, ffn2_w2, w_in, q_norm_w, k_norm_w, attn_sink, gla_gate_w_fwd, gla_gate_b_fwd, gla_gate_w_bwd, gla_gate_b_bwd, gla_norm_w, w_branch_attn, w_branch_gla, w_out):
    tabs = axial_rope_tables(x.shape[1])
    cond = jax.nn.silu(c)
    cond_ctx = jax.nn.silu(c_ctx)
    xc = ctx
    for l in range(DEPTH):
        last = l == DEPTH - 1
        m = adaln(cond, w_mod[l], b_mod[l])
        mc = adaln(cond_ctx, w_mod[l], b_mod[l])
        x = x + 0.5 * m[2] * swiglu(modulate(rmsnorm(x, norm_w[l, 0]), m[0], m[1]), ffn1_w13[l], ffn1_w2[l])
        xc = xc + 0.5 * mc[2] * swiglu(modulate(rmsnorm(xc, norm_w[l, 0]), mc[0], mc[1]), ffn1_w13[l], ffn1_w2[l])
        h = modulate(rmsnorm(x, norm_w[l, 1]), m[3], m[4])
        hc = modulate(rmsnorm(xc, norm_w[l, 1]), mc[3], mc[4])
        y, yc = mixer(h, hc, w_in[l], q_norm_w[l], k_norm_w[l], attn_sink[l],
                      gla_gate_w_fwd[l], gla_gate_b_fwd[l], gla_gate_w_bwd[l], gla_gate_b_bwd[l],
                      gla_norm_w[l], w_branch_attn[l], w_branch_gla[l], w_out[l], tabs, not last)
        x = x + m[5] * y
        x = x + 0.5 * m[8] * swiglu(modulate(rmsnorm(x, norm_w[l, 2]), m[6], m[7]), ffn2_w13[l], ffn2_w2[l])
        if not last:
            xc = xc + mc[5] * yc
            xc = xc + 0.5 * mc[8] * swiglu(modulate(rmsnorm(xc, norm_w[l, 2]), mc[6], mc[7]), ffn2_w13[l], ffn2_w2[l])
    return x


_drawn_inputs = setup_inputs


def setup_inputs(seed=0):
    import zlib

    import numpy as np

    out = dict(_drawn_inputs(seed))
    spreads = {}
    factors = {'norm_w': 6.308,
     'q_norm_w': 8.0,
     'k_norm_w': 8.0,
     'attn_sink': 8.0,
     'gla_gate_w_fwd': 2.927,
     'gla_gate_b_fwd': 8.0,
     'gla_gate_w_bwd': 2.771,
     'gla_gate_b_bwd': 8.0,
     'gla_norm_w': 8.0}
    for name, (base, spread) in spreads.items():
        noise = np.random.default_rng([zlib.crc32(name.encode()), seed]).standard_normal(out[name].shape)
        drawn = base * np.exp(spread * noise) if base else spread * noise
        out[name] = jnp.asarray(drawn.astype(out[name].dtype))
    for name, factor in factors.items():
        out[name] = (out[name] * factor).astype(out[name].dtype)
    return out
```

```python
from contextlib import ExitStack

import numpy as np
import concourse.bass as bass
import concourse.mybir as mybir

F32 = mybir.dt.float32
F32R = mybir.dt.float32r
U8 = mybir.dt.uint8
ALU = mybir.AluOpType
ACT = mybir.ActivationFunctionType
AX = mybir.AxisListType

P = 128
D = 1024
LN_EXP = "natural_log_exp_and_others"
KT = D // P
S = 256
T2 = 2 * S
NTB = T2 // P
DEPTH = 2
N_MOD = 9
EPS = 1e-6
D_FF = 2816
FT = D_FF // P
GROUPS = FT // 2
HEADS = 8
KVH = 2
GRP = HEADS // KVH
SCALE = P ** -0.5
GH = 4
DV = 256
RANK = 16
TEMP = 16.0
UW = 256
UN = KT * UW
COL = dict(ak=0, av=256, gk=512, gv=1024, lr=2048, aq=2080, gq=3104, gr=3616, ga=4640, gg=5664)
LEVELS = [64, 32, 16, 8, 4, 2, 1]
MOD_UNITS = N_MOD * D // UW
MOD_FIRST = 14
FFN_SEGMENTS = [[(11, 2)], [(11, 2)], [(7, 2), (4, 0)], [(11, 0)]]


def schedule():
    start, n = {}, 0

    def take(name, count):
        nonlocal n
        start[name] = n
        n += count

    take("mod", MOD_FIRST)
    for l in range(DEPTH):
        for j in range(2):
            k = 2 * l + j
            if j == 1:
                take(("attn_proj", l), 6)
                take(("branch_a", l), 8)
                take(("gla_proj", l), 1 + 2 * (2 + 4))
                take(("branch_g", l), 8)
                take(("out", l), 4)
            for s, (iters, fill) in enumerate(FFN_SEGMENTS[k]):
                take(("ffn_in", k, s), iters * (2 + fill))
            take(("ffn_out", k), GROUPS)
    start["end"] = n
    return start


START = schedule()
N_UNITS = START["end"]


def hybrid_backbone(nc, a, out):
    ctx = ExitStack()
    with ctx:
        def sb(name, shape, dt=F32, stack=ctx):
            return stack.enter_context(nc.sbuf_tensor(name, shape, dt))

        def sem(name):
            return ctx.enter_context(nc.semaphore(name))

        PS = ctx.enter_context(nc.psum_tensor("PS", [P, 8, 512], F32))
        xT = sb("xT", [P, KT, T2])
        hH = sb("hH", [P, KT, T2], F32R)
        hL = sb("hL", [P, KT, T2], F32R)
        raw = sb("raw", [P, 2, UN])
        WH = sb("WH", [P, 2, UN], F32R)
        WL = sb("WL", [P, 2, UN], F32R)
        mod = sb("mod", [P, DEPTH * N_MOD * KT, 2])
        bmodT = sb("bmodT", [P, DEPTH * N_MOD * KT])
        nwT = sb("nwT", [P, DEPTH * 3 * KT])
        vecT = sb("vecT", [P, 24])
        Q_NORM, K_NORM, BIAS_F, BIAS_B, GLA_NORM = 0, 2, 4, 12, 20
        condT = sb("condT", [P, 2, KT])
        cst = sb("cst", [P, KT, 4], F32R)
        ident = sb("ident", [P, P])
        ones = sb("ones", [P, P])
        swap = sb("swap", [P, P])
        ropeC = sb("ropeC", [P, S])
        ropeS = sb("ropeS", [P, S])
        amask = sb("amask", [P, 2, P])
        lmask = sb("lmask", [P, len(LEVELS), P], U8)
        negsink = sb("negsink", [P, DEPTH * HEADS])
        epsc = sb("epsc", [P, 2])
        gw = sb("gw", [32, 2, GH * P])
        coefA = sb("coefA", [P, KT, 2])
        coefG = sb("coefG", [P, KT, 2])
        rstd = sb("rstd", [P, T2])
        small = sb("small", [P, 64])
        with ExitStack() as r:
            sq = sb("sq", [P, KT, T2], stack=r)
        with ExitStack() as r:
            xin = sb("xin", [P, NTB, D], stack=r)
            rows = sb("rows", [P, 4, P], stack=r)
            xout = sb("xout", [P, S // P, D], stack=r)
            lmask_f = sb("lmask_f", [P, len(LEVELS), P], stack=r)
        with ExitStack() as r:
            hidH = sb("hidH", [P, FT, T2], F32R, stack=r)
            hidL = sb("hidL", [P, FT, T2], F32R, stack=r)
            sg = sb("sg", [P, 2, T2], stack=r)
            hf = sb("hf", [P, 2, T2], stack=r)
        with ExitStack() as r:
            actH = sb("actH", [P, KT, T2], F32R, stack=r)
            actL = sb("actL", [P, KT, T2], F32R, stack=r)
            with ExitStack() as r2:
                kH = sb("kH", [P, KVH, T2], F32R, stack=r2)
                kL = sb("kL", [P, KVH, T2], F32R, stack=r2)
                vH = sb("vH", [P, NTB, UW], F32R, stack=r2)
                vL = sb("vL", [P, NTB, UW], F32R, stack=r2)
                prob = sb("prob", [P, GRP, T2], stack=r2)
                ptH = sb("ptH", [P, NTB, GRP * P], F32R, stack=r2)
                ptL = sb("ptL", [P, NTB, GRP * P], F32R, stack=r2)
                qsq = sb("qsq", [P, 2, T2], stack=r2)
                qrs = sb("qrs", [P, 2, T2], stack=r2)
                qn = sb("qn", [P, 2, T2], stack=r2)
                qt = sb("qt", [P, 2, 2, S], stack=r2)
            with ExitStack() as r2:
                merged = sb("merged", [P, KT, T2], stack=r2)
                with ExitStack() as r3:
                    gate = sb("gate", [P, 2, T2], stack=r3)
                    mpart = sb("mpart", [P, 2, T2], stack=r3)
                with ExitStack() as r3:
                    lrT = sb("lrT", [32, T2], stack=r3)
                    gkq = sb("gkq", [P, 2, 2, T2], stack=r3)
                    gvn = sb("gvn", [P, NTB, DV], stack=r3)
                    sgr = sb("sgr", [P, 2, T2], stack=r3)
                    b2 = sb("b2", [P, 2, T2], stack=r3)
                    dq = sb("dq", [P, 2, 2, T2], stack=r3)
                    A = sb("A", [P, T2], stack=r3)
                    khn = sb("khn", [P, 2, T2], stack=r3)
                    on = khn
                    st = sb("st", [P, 6, DV], stack=r3)
                    dec = sb("dec", [P, 2, NTB], stack=r3)

        const_in = sem("const_in")
        x_in = sem("x_in")
        rows_in = sem("rows_in")
        sink_in = sem("sink_in")
        gw_in = sem("gw_in")
        gw_zero = sem("gw_zero")
        out_in_dram = sem("out_in_dram")
        raw_in = [sem("raw_in0"), sem("raw_in1")]
        wh_ready = sem("wh_ready")
        wl_ready = sem("wl_ready")
        unit_done = sem("unit_done")
        vec_t = sem("vec_t")
        vec_ready = sem("vec_ready")
        cond_silu = sem("cond_silu")
        cst_hi = sem("cst_hi")
        cst_ready = sem("cst_ready")
        x_t = sem("x_t")
        x_ready = sem("x_ready")
        eps_ready = sem("eps_ready")
        mod_part = sem("mod_part")
        mod_done = sem("mod_done")
        coef_ready = sem("coef_ready")
        sq_done = sem("sq_done")
        ss_done = sem("ss_done")
        ln_done = sem("ln_done")
        rstd_done = sem("rstd_done")
        xn_done = sem("xn_done")
        hf_done = sem("hf_done")
        h_hi = sem("h_hi")
        h_ready = sem("h_ready")
        silu_done = sem("silu_done")
        gated = sem("gated")
        hid_hi = sem("hid_hi")
        hid_lo = sem("hid_lo")
        v_hi = sem("v_hi")
        v_ready = sem("v_ready")
        qk_sq = sem("qk_sq")
        qk_ss = sem("qk_ss")
        qk_ln = sem("qk_ln")
        qk_rs = sem("qk_rs")
        qk_n = sem("qk_n")
        qk_swap = sem("qk_swap")
        qk_parts = sem("qk_parts")
        qk_rot = sem("qk_rot")
        qk_hi = sem("qk_hi")
        qk_ready = sem("qk_ready")
        at_score = sem("at_score")
        at_masked = sem("at_masked")
        at_max = sem("at_max")
        at_negmax = sem("at_negmax")
        ident_in = sem("ident_in")
        lmask_in = sem("lmask_in")
        lmask_ready = sem("lmask_ready")
        at_nm = sem("at_nm")
        at_exp = sem("at_exp")
        at_den = sem("at_den")
        at_rden = sem("at_rden")
        at_prob = sem("at_prob")
        at_t = sem("at_t")
        at_pth = sem("at_pth")
        at_ptl = sem("at_ptl")
        at_out = sem("at_out")
        at_yh = sem("at_yh")
        at_yl = sem("at_yl")
        sig_done = sem("sig_done")
        br_part = sem("br_part")
        br_done = sem("br_done")
        m_hi = sem("m_hi")
        m_ready = sem("m_ready")
        lr_ready = sem("lr_ready")
        kq_ready = sem("kq_ready")
        v_gla = sem("v_gla")
        r_ready = sem("r_ready")
        lg_done = sem("lg_done")
        lg_abs = sem("lg_abs")
        lg_exp = sem("lg_exp")
        lg_ln = sem("lg_ln")
        lg_min = sem("lg_min")
        g_ready = sem("g_ready")
        b_ready = sem("b_ready")
        lv_diff = sem("lv_diff")
        lv_exp = sem("lv_exp")
        lv_prod = sem("lv_prod")
        lv_mm = sem("lv_mm")
        lv_acc = sem("lv_acc")
        diag_mm = sem("diag_mm")
        diag_ready = sem("diag_ready")
        kh_ready = sem("kh_ready")
        u_done = sem("u_done")
        st_step = sem("st_step")
        o_done = sem("o_done")
        o_sq = sem("o_sq")
        o_ln = sem("o_ln")
        o_rs = sem("o_rs")
        on_ready = sem("on_ready")
        ot_done = sem("ot_done")
        yg_f = sem("yg_f")
        yg_hi = sem("yg_hi")
        yg_ready = sem("yg_ready")
        out_t = sem("out_t")
        out_ready = sem("out_ready")

        wmod_d = [a["w_mod"][l].rearrange("(k p) c -> p k c", p=P) for l in range(DEPTH)]
        win_d = [a["w_in"][l].rearrange("(k p) c -> p k c", p=P) for l in range(DEPTH)]
        w13_d = [a[w][l].rearrange("(k p) c -> p k c", p=P) for l in range(DEPTH) for w in ("ffn1_w13", "ffn2_w13")]
        w2_d = [a[w][l].rearrange("(k p) c -> p k c", p=P) for l in range(DEPTH) for w in ("ffn1_w2", "ffn2_w2")]
        wba_d = [a["w_branch_attn"][l].rearrange("(k p) c -> p k c", p=P) for l in range(DEPTH)]
        wbg_d = [a["w_branch_gla"][l].rearrange("(k p) c -> p k c", p=P) for l in range(DEPTH)]
        wout_d = [a["w_out"][l].rearrange("(k p) c -> p k c", p=P) for l in range(DEPTH)]

        def tokens(k):
            return T2 if k < 3 else S

        def qtokens(l):
            return T2 if l == 0 else S

        SETS = [[(kv, qb) for kv in range(KVH) for qb in range(qtokens(l) // P)] for l in range(DEPTH)]
        set0 = [0, len(SETS[0])]
        tile0 = 10

        def keys(qb):
            return (0, NTB) if qb < 2 else (S, 2)

        def nbase(name):
            return START[name]

        def mods_before_norm(n):
            l, j = divmod(n, 3)
            if n == 0:
                return 12
            if n < 3:
                return MOD_UNITS
            return MOD_UNITS + (22 if n == 3 else MOD_UNITS)

        MODQ0 = {(0, 0): MOD_FIRST, (1, 0): MOD_UNITS, (2, 0): MOD_UNITS + 22}

        block = ctx.enter_context(nc.Block())

        @block.sync
        def _(sp):
            sp.dma_start(rows[0:16, 2, :], a["cond_rows"]).then_inc(rows_in, 16)
            sp.dma_start(ident[:], a["c_ident"]).then_inc(ident_in, 16)
            sp.dma_start(rows[0:72, 0, :], a["b_mod"][0].rearrange("(r p) -> r p", p=P)).then_inc(rows_in, 16)
            sp.dma_start(rows[0:72, 1, :], a["b_mod"][1].rearrange("(r p) -> r p", p=P)).then_inc(rows_in, 16)
            sp.dma_start(rows[0:48, 3, :], a["norm_w"].rearrange("l j (r p) -> (l j r) p", p=P)).then_inc(rows_in, 16)
            for at, name in ((Q_NORM, "q_norm_w"), (K_NORM, "k_norm_w"), (BIAS_F, "gla_gate_b_fwd"),
                             (BIAS_B, "gla_gate_b_bwd"), (GLA_NORM, "gla_norm_w")):
                src = a[name].rearrange("l (r p) -> (l r) p", p=P)
                sp.dma_start(rows[64 + at:64 + at + src.shape[0], 3, :], src).then_inc(rows_in, 16)

            def load(n, slot, view, shape, pair=0):
                if pair == 0 and not (isinstance(n, int) and n < 2):
                    sp.wait_ge(wl_ready, n - 1)
                if pair == 1:
                    sp.wait_ge(wl_ready, n)
                dst = raw[:, slot, :].rearrange("p (k c) -> p k c", k=shape)
                sp.dma_start(dst, view).then_inc(raw_in[slot], 16)

            s0 = START["mod"]
            load(0, 0, wmod_d[0][:, :, 0:UW], KT)
            load(1, 1, wmod_d[0][:, :, UW:2 * UW], KT)
            sp.dma_start(xin[:, 0:2, :], a["x"][0].rearrange("(t p) d -> p t d", p=P)).then_inc(x_in, 16)
            sp.dma_start(xin[:, 2:4, :], a["ctx"][0].rearrange("(t p) d -> p t d", p=P)).then_inc(x_in, 16)
            for dst, name in ((ones, "c_ones"), (swap, "c_swap"), (ropeC, "c_cos"), (ropeS, "c_sin")):
                sp.dma_start(dst[:], a[name]).then_inc(const_in, 16)
            sp.dma_start(amask[:], a["c_amask"]).then_inc(const_in, 16)
            sp.dma_start(lmask_f[:], a["c_lmask"]).then_inc(lmask_in, 16)
            sp.dma_start(negsink[:], a["attn_sink"].rearrange("l h -> (l h)").partition_broadcast(P)).then_inc(sink_in, 16)
            with sp.Fori(1, MOD_FIRST // 2) as i:
                for s in range(2):
                    load(2 * i + s, s, wmod_d[0][:, :, bass.ds(sp.snap((2 * i + s) * UW), UW)], KT)

            def load_gates(l):
                sp.wait_ge(gw_zero, 1)
                if l:
                    sp.wait_ge(lg_done, GH * l)
                sp.dma_start(gw[0:RANK, 0, :], a["gla_gate_w_fwd"][l]).then_inc(gw_in, 16)
                sp.dma_start(gw[RANK:2 * RANK, 1, :], a["gla_gate_w_bwd"][l]).then_inc(gw_in, 16)

            for k in range(4):
                l = k // 2
                if k % 2 == 1:
                    n = START[("attn_proj", l)]
                    cols = [COL["av"], COL["ak"]] + [COL["aq"] + j * UW for j in range(4)]
                    for j, c in enumerate(cols):
                        load(n + j, (n + j) % 2, win_d[l][:, :, c:c + UW], KT)
                    n = START[("branch_a", l)]
                    with sp.Fori(0, 4) as i:
                        load(n + 2 * i, n % 2, win_d[l][:, :, bass.ds(sp.snap(COL["ga"] + i * UW), UW)], KT, 1)
                        load(n + 2 * i + 1, (n + 1) % 2, wba_d[l][:, :, bass.ds(sp.snap(i * UW), UW)], KT, 2)
                    load_gates(l)
                    n = START[("gla_proj", l)]
                    cols = [COL["lr"]]
                    for pr in range(2):
                        cols += [COL["gk"] + pr * UW, COL["gq"] + pr * UW]
                        for h in (2 * pr, 2 * pr + 1):
                            cols += [COL["gv"] + h * UW, COL["gr"] + h * UW]
                    for j, c in enumerate(cols):
                        load(n + j, (n + j) % 2, win_d[l][:, :, c:c + UW], KT)
                    n = START[("branch_g", l)]
                    with sp.Fori(0, 4) as i:
                        load(n + 2 * i, n % 2, win_d[l][:, :, bass.ds(sp.snap(COL["gg"] + i * UW), UW)], KT, 1)
                        load(n + 2 * i + 1, (n + 1) % 2, wbg_d[l][:, :, bass.ds(sp.snap(i * UW), UW)], KT, 2)
                    n = START[("out", l)]
                    with sp.Fori(0, 2) as i:
                        for s in range(2):
                            load(n + 2 * i + s, (n + s) % 2, wout_d[l][:, :, bass.ds(sp.snap((2 * i + s) * UW), UW)], KT)
                g0 = 0
                for s, (iters, fill) in enumerate(FFN_SEGMENTS[k]):
                    n, per = START[("ffn_in", k, s)], 2 + fill
                    with sp.Fori(0, iters) as i:
                        load(n + per * i, n % 2, w13_d[k][:, :, bass.ds(sp.snap(D_FF + (i + g0) * UW), UW)], KT, 1)
                        load(n + per * i + 1, (n + 1) % 2, w13_d[k][:, :, bass.ds(sp.snap((i + g0) * UW), UW)], KT, 2)
                        for f in range(fill):
                            q0 = MODQ0[(k, s)]
                            lm, c0 = divmod(q0, MOD_UNITS)
                            load(n + per * i + 2 + f, (n + f) % 2,
                                 wmod_d[lm][:, :, bass.ds(sp.snap((c0 + f + fill * i) * UW), UW)], KT)
                    g0 += iters
                n = START[("ffn_out", k)]
                with sp.Fori(0, GROUPS // 2) as i:
                    for s in range(2):
                        load(n + 2 * i + s, (n + s) % 2, w2_d[k][:, bass.ds(sp.snap((2 * i + s) * 2), 2), :], 2)
                load(n + GROUPS - 1, (n + GROUPS - 1) % 2, w2_d[k][:, FT - 2:FT, :], 2)

            sp.wait_ge(out_ready, 2)
            sp.dma_start(out[0].rearrange("(t p) d -> p t d", p=P), xout[:]).then_inc(out_in_dram, 16)
            sp.wait_ge(out_in_dram, 16)

        @block.gpsimd
        def _(pool):
            nc.gpsimd.memset(epsc[:, 0:1], EPS)
            nc.gpsimd.memset(epsc[:, 1:2], 1.0).then_inc(eps_ready, 1)
            nc.gpsimd.memset(gw[:], 0.0).then_inc(gw_zero, 1)

            def norm(n, T):
                pool.wait_ge(rstd_done, n + 1)
                for kt in range(KT):
                    nc.gpsimd.tensor_tensor(sq[:, kt, 0:T], xT[:, kt, 0:T], rstd[:, 0:T], ALU.mult).then_inc(xn_done, 1)

            def diffs(l, q):
                T = qtokens(l)
                pool.wait_ge(b_ready, q + 1)
                for d, at in ((0, P - 1), (1, 0)):
                    b = b2[:, d, :].rearrange("p (n m) -> p n m", m=P)
                    ins = nc.gpsimd.tensor_tensor(
                        dq[:, 0, d, :].rearrange("p (n m) -> p n m", m=P),
                        b[:, :, at:at + 1].to_broadcast([P, NTB, P]), b, ALU.subtract)
                ins.then_inc(lv_diff, 1)
                for v, m in enumerate(LEVELS):
                    i = v + 1
                    if i >= 2:
                        pool.wait_ge(lv_mm, 8 * q + i - 1)
                    elif q:
                        pool.wait_ge(yg_ready, q)
                    nb = T // (2 * m)
                    bv = b2[:, :, 0:T].rearrange("p d (n s m) -> p d n s m", s=2, m=m)
                    ov = dq[:, i % 2, :, 0:T].rearrange("p d (n s m) -> p d n s m", s=2, m=m)
                    fm = bv[:, 0, :, 0, m - 1:m].to_broadcast([P, nb, m])
                    bm = bv[:, 1, :, 1, 0:1].to_broadcast([P, nb, m])
                    nc.gpsimd.tensor_tensor(ov[:, 0, :, 0, :], fm, bv[:, 0, :, 0, :], ALU.subtract)
                    nc.gpsimd.tensor_tensor(ov[:, 0, :, 1, :], bm, bv[:, 1, :, 1, :], ALU.subtract)
                    nc.gpsimd.tensor_tensor(ov[:, 1, :, 1, :], bv[:, 0, :, 1, :], fm, ALU.subtract)
                    nc.gpsimd.tensor_tensor(ov[:, 1, :, 0, :], bv[:, 1, :, 0, :], bm, ALU.subtract).then_inc(lv_diff, 1)

            for l in range(DEPTH):
                norm(3 * l, T2)
                norm(3 * l + 1, T2)
                for h in range(GH):
                    diffs(l, GH * l + h)
                norm(3 * l + 2, tokens(2 * l + 1))

        @block.scalar
        def _(act):
            def prep(n, par):
                if isinstance(n, int) and n >= N_UNITS:
                    return
                act.wait_ge(raw_in[par], (n // 2 + 1) * 16 if isinstance(n, int) else 8 * (n - par) + 16)
                if not (isinstance(n, int) and n < 2):
                    act.wait_ge(unit_done, n - 1)
                nc.scalar.copy(WH[:, par, :], raw[:, par, :]).then_inc(wh_ready, 1)

            act.wait_ge(vec_t, 3)
            nc.scalar.activation(condT[:], PS[:, 7, 0:16].rearrange("p (c k) -> p c k", c=2), ACT.Silu).then_inc(cond_silu, 1)
            act.wait_ge(cond_silu, 1)
            nc.scalar.copy(cst[:, :, 0:2].rearrange("p k c -> p c k"), condT[:]).then_inc(cst_hi, 1)
            prep(0, 0)
            act.wait_ge(eps_ready, 1)
            with act.Fori(0, MOD_FIRST // 2) as i:
                for s in range(2):
                    prep(2 * i + s + 1, (s + 1) % 2)

            def norm(n, T, width=D):
                nc.scalar.preload_act_table_set(LN_EXP)
                for kt in range(KT):
                    act.wait_ge(x_ready, KT * n + kt + 1)
                    nc.scalar.activation(sq[:, kt, 0:T], xT[:, kt, 0:T], ACT.Square).then_inc(sq_done, 1)
                act.wait_ge(ss_done, n + 1)
                nc.scalar.activation(rstd[:, 0:T], PS[:, 0, 0:T], ACT.Ln, bias=epsc[:, 0:1], scale=1.0 / width).then_inc(ln_done, 1)
                act.wait_ge(ln_done, n + 1)
                nc.scalar.activation(rstd[:, 0:T], rstd[:, 0:T], ACT.Exp, scale=-0.5).then_inc(rstd_done, 1)
                for kt in range(KT):
                    act.wait_ge(hf_done, KT * n + kt + 1)
                    nc.scalar.copy(hH[:, kt, 0:T], sq[:, kt, 0:T]).then_inc(h_hi, 1)

            def ffn(k):
                T, g0 = tokens(k), GROUPS * k
                done = 0
                nc.scalar.preload_act_table(ACT.Silu)
                for s, (iters, fill) in enumerate(FFN_SEGMENTS[k]):
                    n, per = START[("ffn_in", k, s)], 2 + fill
                    gb = g0 + done
                    with act.Fori(0, iters) as i:
                        u = n + per * i
                        prep(u + 1, (n + 1) % 2)
                        act.wait_ge(unit_done, u + 1)
                        act.wait_ge(gated, gb + i)
                        nc.scalar.activation(sg[:, :, 0:T], PS[:, 0:2, 0:T], ACT.Silu).then_inc(silu_done, 1)
                        prep(u + 2, n % 2)
                        act.wait_ge(gated, gb + i + 1)
                        nc.scalar.copy(hidH[:, bass.ds(2 * (i + done), 2), 0:T], hf[:, :, 0:T]).then_inc(hid_hi, 1)
                        for f in range(fill):
                            prep(u + 3 + f, (n + 1 + f) % 2)
                    done += iters
                n = START[("ffn_out", k)]
                with act.Fori(0, GROUPS // 2) as i:
                    for s in range(2):
                        prep(n + 2 * i + s + 1, (n + s + 1) % 2)
                prep(n + GROUPS, (n + GROUPS) % 2)

            def qk_tiles(l, j):
                return [(tile0 * l + 2 * (j - 1) + e, T2 if j == 1 else qtokens(l)) for e in range(2)]

            def attn_proj(l):
                n = START[("attn_proj", l)]
                prep(n + 1, (n + 1) % 2)
                act.wait_ge(unit_done, n + 1)
                nc.scalar.copy(vH[:], PS[:, 0:2, :].rearrange("p a (b c) -> p (a b) c", c=UW)).then_inc(v_hi, 1)

                def squares(j):
                    act.wait_ge(unit_done, n + j + 1)
                    for e, (t, T) in enumerate(qk_tiles(l, j)):
                        if t >= 2:
                            act.wait_ge(qk_ss, t - 1)
                        nc.scalar.activation(qsq[:, e, 0:T], PS[:, 2 * (j % 3) + e, 0:T], ACT.Square).then_inc(qk_sq, 1)

                def rsq(j):
                    for e, (t, T) in enumerate(qk_tiles(l, j)):
                        act.wait_ge(qk_ss, t + 1)
                        if t >= 2:
                            act.wait_ge(qk_n, t - 1)
                        nc.scalar.activation(qrs[:, e, 0:T], PS[:, 6 + e, 0:T], ACT.Ln, bias=epsc[:, 0:1], scale=1.0 / P).then_inc(qk_ln, 1)
                    for e, (t, T) in enumerate(qk_tiles(l, j)):
                        act.wait_ge(qk_ln, t + 1)
                        nc.scalar.activation(qrs[:, e, 0:T], qrs[:, e, 0:T], ACT.Exp, scale=-0.5).then_inc(qk_rs, 1)

                def split(j):
                    for e, (t, T) in enumerate(qk_tiles(l, j)):
                        act.wait_ge(qk_rot, t + 1)
                        dst = kH[:, e, 0:T] if j == 1 else actH[:, 2 * (j - 2) + e, 0:T]
                        nc.scalar.copy(dst, qn[:, e, 0:T]).then_inc(qk_hi, 1)

                for j in range(1, 8):
                    if j < 6:
                        prep(n + j + 1, (n + j + 1) % 2)
                        squares(j)
                    if 1 <= j - 1 < 6:
                        rsq(j - 1)
                    if 1 <= j - 2 < 6:
                        split(j - 2)

            def attention(l):
                A0, sets = set0[l], SETS[l]

                def exps(i):
                    kv, qb = sets[i]
                    k0, nkb = keys(qb)
                    act.wait_ge(at_nm, A0 + i + 1)
                    if A0 + i:
                        act.wait_ge(at_t, A0 + i)
                    for g in range(GRP):
                        nc.scalar.activation(prob[:, g, 0:nkb * P], PS[:, g, 0:nkb * P], ACT.Exp, bias=small[:, 8 + g:9 + g],
                                             scale=SCALE, accum_out=small[:, 16 + g:17 + g])
                    nc.scalar.activation(small[:, 24:28], small[:, 12:16], ACT.Exp).then_inc(at_exp, 1)

                exps(0)
                for i, (kv, qb) in enumerate(sets):
                    k0, nkb = keys(qb)
                    act.wait_ge(at_t, A0 + i + 1)
                    nc.scalar.copy(ptH[:, 0:nkb, :], PS[:, 4:4 + nkb, :]).then_inc(at_pth, 1)
                    if i + 1 < len(sets):
                        exps(i + 1)
                    act.wait_ge(at_out, A0 + i + 1)
                    nc.scalar.copy(actH[:, GRP * kv:GRP * (kv + 1), qb * P:(qb + 1) * P],
                                   PS[:, 4, :].rearrange("p (g q) -> p g q", g=GRP)).then_inc(at_yh, 1)

            def branch(l, which):
                T = qtokens(l)
                n = START[(("branch_a", "branch_g")[which], l)]
                c0 = 8 * l + 4 * which
                nc.scalar.preload_act_table(ACT.Sigmoid)
                with act.Fori(0, 4) as i:
                    prep(n + 2 * i + 1, (n + 1) % 2)
                    act.wait_ge(unit_done, n + 2 * i + 1)
                    act.wait_ge(br_done, c0 + i)
                    nc.scalar.activation(gate[:, :, 0:T], PS[:, 0:2, 0:T], ACT.Sigmoid).then_inc(sig_done, 1)
                    prep(n + 2 * i + 2, n % 2)

            def gla_head(l, h, n):
                q, T = GH * l + h, qtokens(l)
                nb, c = T // P, 9 * (GH * l + h)
                nc.scalar.preload_act_table_set(LN_EXP)
                act.wait_ge(lg_done, q + 1)
                if q:
                    act.wait_ge(lv_exp, c)
                for d, at in ((0, BIAS_F), (1, BIAS_B)):
                    act.wait_ge(lg_min, 2 * q + d + 1)
                    nc.scalar.activation(b2[:, d, :], PS[:, 6 + d, :], ACT.Abs, bias=vecT[:, at + GH * l + h:at + GH * l + h + 1]).then_inc(lg_abs, 1)
                act.wait_ge(lg_abs, 2 * q + 2)
                nc.scalar.activation(b2[:], b2[:], ACT.Exp, scale=-1.0).then_inc(lg_exp, 1)
                act.wait_ge(lg_exp, q + 1)
                nc.scalar.activation(b2[:], b2[:], ACT.Ln, bias=epsc[:, 1:2]).then_inc(lg_ln, 1)
                prep(n + 1, (n + 1) % 2)
                act.wait_ge(b_ready, q + 1)
                bv = b2[:].rearrange("p d (n m) -> p d n m", m=P)
                if q:
                    act.wait_ge(st_step, 6 * q)
                nc.scalar.activation(dec[:, 0, :], bv[:, 0, :, P - 1], ACT.Exp, scale=1.0 / TEMP)
                nc.scalar.activation(dec[:, 1, :], bv[:, 1, :, 0], ACT.Exp, scale=1.0 / TEMP)
                act.wait_ge(lv_diff, 8 * q + 1)
                nc.scalar.activation(dq[:, 0, :, :], dq[:, 0, :, :], ACT.Exp, scale=1.0 / TEMP).then_inc(lv_exp, 1)
                act.wait_ge(diag_mm, q + 1)
                if q:
                    act.wait_ge(o_done, q)
                nc.scalar.activation(A[:, 0:T], PS[:, 5, 0:T], ACT.Copy, scale=2.0).then_inc(diag_ready, 1)
                for i in range(1, 8):
                    act.wait_ge(lv_diff, 8 * q + i + 1)
                    nc.scalar.activation(dq[:, i % 2, :, 0:T], dq[:, i % 2, :, 0:T], ACT.Exp, scale=1.0 / TEMP).then_inc(lv_exp, 1)
                    if i == 1:
                        act.wait_ge(lv_mm, 8 * q + 1)
                        nc.scalar.copy(khn[:], PS[:, 6:8, :]).then_inc(kh_ready, 1)
                        act.wait_ge(unit_done, n + 1)
                        nc.scalar.copy(gvn[:], PS[:, 0:2, :].rearrange("p a (b c) -> p (a b) c", c=DV)).then_inc(v_gla, 1)
                    if i == 3:
                        prep(n + 2, n % 2)
                act.wait_ge(lv_mm, 8 * q + 7)
                nc.scalar.activation(dq[:, 0, :, 0:T], b2[:, :, 0:T], ACT.Exp, scale=1.0 / TEMP).then_inc(lv_exp, 1)
                act.wait_ge(unit_done, n + 2)
                if q:
                    act.wait_ge(yg_f, 2 * q)
                nc.scalar.activation(sgr[:, :, 0:T], PS[:, 2:4, 0:T], ACT.Silu).then_inc(r_ready, 1)
                nc.scalar.preload_act_table_set(LN_EXP)
                act.wait_ge(o_done, q + 1)
                for b in range(nb):
                    nc.scalar.activation(khn[:, b // 2, b % 2 * DV:b % 2 * DV + DV], PS[:, 6 + b // 2, b % 2 * DV:b % 2 * DV + DV],
                                         ACT.Square, accum_out=small[:, 32 + b:33 + b]).then_inc(o_sq, 1)
                oq = o_sq_base(l, h) + nb
                act.wait_ge(o_sq, oq)
                nc.scalar.activation(small[:, 36:36 + nb], small[:, 32:32 + nb], ACT.Ln, bias=epsc[:, 0:1], scale=1.0 / DV).then_inc(o_ln, 1)
                act.wait_ge(o_ln, q + 1)
                nc.scalar.activation(small[:, 40:40 + nb], small[:, 36:36 + nb], ACT.Exp, scale=-0.5).then_inc(o_rs, 1)
                for e in range(2):
                    act.wait_ge(yg_f, 2 * q + e + 1)
                    nc.scalar.copy(actH[:, 2 * h + e, 0:T], dq[:, 1, e, 0:T]).then_inc(yg_hi, 1)

            def o_sq_base(l, h):
                return (GH * NTB + 2 * h) if l else NTB * h

            def gla(l):
                n = START[("gla_proj", l)]
                prep(n + 1, (n + 1) % 2)
                act.wait_ge(unit_done, n + 1)
                nc.scalar.copy(lrT[:], PS[0:32, 0, :]).then_inc(lr_ready, 1)
                u = n + 1
                for pr in range(2):
                    for z in range(2):
                        T = T2 if z == 0 else qtokens(l)
                        prep(u + 1, (u + 1) % 2)
                        act.wait_ge(unit_done, u + 1)
                        if 2 * l + pr:
                            act.wait_ge(lv_prod, 9 * (GH * l + 2 * pr))
                            act.wait_ge(diag_mm, GH * l + 2 * pr)
                        nc.scalar.activation(gkq[:, :, z, 0:T], PS[:, 2 * z:2 * z + 2, 0:T], ACT.Copy,
                                             scale=1.0 if z == 0 else SCALE).then_inc(kq_ready, 1)
                        u += 1
                    for h in (2 * pr, 2 * pr + 1):
                        gla_head(l, h, u)
                        u += 2

            def merge_split(l):
                T = qtokens(l)
                act.wait_ge(br_done, 8 * (l + 1))
                for kt in range(KT):
                    nc.scalar.copy(actH[:, kt, 0:T], merged[:, kt, 0:T]).then_inc(m_hi, 1)

            def out_proj(l):
                n = START[("out", l)]
                for j in range(4):
                    prep(n + j + 1, (n + j + 1) % 2)

            for l in range(DEPTH):
                norm(3 * l, T2)
                ffn(2 * l)
                norm(3 * l + 1, T2)
                attn_proj(l)
                attention(l)
                branch(l, 0)
                gla(l)
                branch(l, 1)
                merge_split(l)
                out_proj(l)
                norm(3 * l + 2, tokens(2 * l + 1))
                ffn(2 * l + 1)

        @block.vector
        def _(dve):
            def prep(n, par):
                if isinstance(n, int) and n >= N_UNITS:
                    return
                dve.wait_ge(wh_ready, n + 1)
                nc.vector.tensor_tensor(WL[:, par, :], raw[:, par, :], WH[:, par, :].bitcast(F32), ALU.subtract).then_inc(wl_ready, 1)

            dve.wait_ge(vec_t, 1)
            nc.vector.tensor_copy(bmodT[:, 0:72], PS[:, 5, 0:72])
            nc.vector.tensor_copy(bmodT[:, 72:144], PS[:, 5, 128:200])
            dve.wait_ge(vec_t, 2)
            nc.vector.tensor_copy(nwT[:], PS[:, 6, 0:48])
            nc.vector.tensor_copy(vecT[:], PS[:, 6, 64:88]).then_inc(vec_ready, 1)
            dve.wait_ge(cst_hi, 1)
            nc.vector.tensor_tensor(cst[:, :, 2:4].rearrange("p k c -> p c k"), condT[:],
                                    cst[:, :, 0:2].rearrange("p k c -> p c k").bitcast(F32), ALU.subtract).then_inc(cst_ready, 1)
            prep(0, 0)
            for kt in range(KT):
                dve.wait_ge(x_t, kt + 1)
                nc.vector.tensor_copy(xT[:, kt, :], PS[:, kt, :]).then_inc(x_ready, 1)
            dve.wait_ge(sink_in, 16)
            nc.vector.tensor_scalar(negsink[:], negsink[:], -1.0, None, ALU.mult)
            dve.wait_ge(lmask_in, 16)
            nc.vector.tensor_copy(lmask[:], lmask_f[:]).then_inc(lmask_ready, 1)

            def mod_post(n, q, par):
                dve.wait_ge(unit_done, n + 1)
                dve.wait_ge(mod_done, q)
                ps = PS[:, 4 + par, 0:8].rearrange("p (m c) -> p m c", m=2)
                tmp = small[:, 48:52].rearrange("p (m c) -> p m c", m=2)
                nc.vector.tensor_tensor(tmp, ps[:, :, 0:2], bmodT[:, bass.ds(2 * q, 2)].unsqueeze(2).to_broadcast([P, 2, 2]), ALU.add).then_inc(mod_part, 1)
                dve.wait_ge(mod_part, q + 1)
                nc.vector.tensor_tensor(mod[:, bass.ds(2 * q, 2), :], tmp, ps[:, :, 2:4], ALU.add).then_inc(mod_done, 1)

            with dve.Fori(0, MOD_FIRST // 2) as i:
                for s in range(2):
                    prep(2 * i + s + 1, (s + 1) % 2)
                    mod_post(2 * i + s, 2 * i + s, s)

            def modcol(l, j):
                return mod[:, (N_MOD * l + j) * KT:(N_MOD * l + j + 1) * KT, :]

            def norm(n, T):
                l, j = divmod(n, 3)
                dve.wait_ge(mod_done, mods_before_norm(n))
                dve.wait_ge(x_ready, KT * (n + 1))
                nw = nwT[:, n * KT:(n + 1) * KT].unsqueeze(2).to_broadcast([P, KT, 2])
                nc.vector.scalar_tensor_tensor(coefA[:], modcol(l, 3 * j + 1), 1.0, nw, ALU.add, ALU.mult)
                nc.vector.tensor_scalar(coefG[:], modcol(l, 3 * j + 2), 1.0 if j == 1 else 0.5, None, ALU.mult).then_inc(coef_ready, 1)
                dve.wait_ge(coef_ready, n + 1)
                shift = modcol(l, 3 * j)

                def lo(kt):
                    dve.wait_ge(h_hi, KT * n + kt + 1)
                    nc.vector.tensor_tensor(hL[:, kt, 0:T], sq[:, kt, 0:T], hH[:, kt, 0:T].bitcast(F32), ALU.subtract).then_inc(h_ready, 1)

                for kt in range(KT):
                    dve.wait_ge(xn_done, KT * n + kt + 1)
                    for c in range(T // S):
                        ins = nc.vector.tensor_scalar(sq[:, kt, c * S:(c + 1) * S], sq[:, kt, c * S:(c + 1) * S],
                                                      coefA[:, kt, c:c + 1], shift[:, kt, c:c + 1], ALU.mult, ALU.add)
                    ins.then_inc(hf_done, 1)
                    if kt:
                        lo(kt - 1)
                lo(KT - 1)

            def residual(n, T):
                for kt in range(KT):
                    for c in range(T // S):
                        ins = nc.vector.scalar_tensor_tensor(xT[:, kt, c * S:(c + 1) * S], PS[:, kt, c * S:(c + 1) * S],
                                                             coefG[:, kt, c:c + 1], xT[:, kt, c * S:(c + 1) * S], ALU.mult, ALU.add)
                    ins.then_inc(x_ready, 1)

            def ffn(k):
                T, g0 = tokens(k), GROUPS * k
                done = 0
                for s, (iters, fill) in enumerate(FFN_SEGMENTS[k]):
                    n, per = START[("ffn_in", k, s)], 2 + fill
                    gb = g0 + done
                    with dve.Fori(0, iters) as i:
                        u = n + per * i
                        prep(u + 1, (n + 1) % 2)
                        prep(u + 2, n % 2)
                        dve.wait_ge(unit_done, u + 2)
                        dve.wait_ge(silu_done, gb + i + 1)
                        dve.wait_ge(hid_lo, gb + i)
                        nc.vector.tensor_tensor(hf[:, :, 0:T], sg[:, :, 0:T], PS[:, 2:4, 0:T], ALU.mult).then_inc(gated, 1)
                        if fill:
                            prep(u + 3, (n + 1) % 2)
                        dve.wait_ge(hid_hi, gb + i + 1)
                        nc.vector.tensor_tensor(hidL[:, bass.ds(2 * (i + done), 2), 0:T], hf[:, :, 0:T],
                                                hidH[:, bass.ds(2 * (i + done), 2), 0:T].bitcast(F32), ALU.subtract).then_inc(hid_lo, 1)
                        for f in range(fill):
                            if f:
                                prep(u + 3 + f, (n + 1 + f) % 2)
                            mod_post(u + 2 + f, MODQ0[(k, s)] + fill * i + f, (n + f) % 2)
                    done += iters
                n = START[("ffn_out", k)]
                with dve.Fori(0, GROUPS // 2) as i:
                    for s in range(2):
                        prep(n + 2 * i + s + 1, (n + s + 1) % 2)
                prep(n + GROUPS, (n + GROUPS) % 2)
                dve.wait_ge(unit_done, n + GROUPS)
                residual(None, T)

            def qk_tiles(l, j):
                return [(tile0 * l + 2 * (j - 1) + e, T2 if j == 1 else qtokens(l)) for e in range(2)]

            def attn_proj(l):
                n = START[("attn_proj", l)]
                prep(n + 1, (n + 1) % 2)
                dve.wait_ge(v_hi, l + 1)
                nc.vector.tensor_tensor(vL[:], PS[:, 0:2, :].rearrange("p a (b c) -> p (a b) c", c=UW),
                                        vH[:].bitcast(F32), ALU.subtract).then_inc(v_ready, 1)

                def normed(j):
                    for e, (t, T) in enumerate(qk_tiles(l, j)):
                        dve.wait_ge(qk_rs, t + 1)
                        if t >= 2:
                            dve.wait_ge(qk_ready, t - 1)
                        w = vecT[:, K_NORM + l:K_NORM + l + 1] if j == 1 else vecT[:, Q_NORM + l:Q_NORM + l + 1]
                        nc.vector.scalar_tensor_tensor(qn[:, e, 0:T], PS[:, 2 * (j % 3) + e, 0:T], w, qrs[:, e, 0:T],
                                                       ALU.mult, ALU.mult).then_inc(qk_n, 1)

                def rotate(j):
                    for e, (t, T) in enumerate(qk_tiles(l, j)):
                        dve.wait_ge(qk_swap, t + 1)
                        nc.vector.tensor_tensor(qt[:, e, 0, :], qn[:, e, 0:S], ropeC[:], ALU.mult)
                        nc.vector.tensor_tensor(qt[:, e, 1, :], PS[:, 2 * (j % 3) + e, 0:S], ropeS[:], ALU.mult).then_inc(qk_parts, 1)
                    for e, (t, T) in enumerate(qk_tiles(l, j)):
                        dve.wait_ge(qk_parts, t + 1)
                        nc.vector.tensor_tensor(qn[:, e, 0:S], qt[:, e, 0, :], qt[:, e, 1, :], ALU.add).then_inc(qk_rot, 1)
                    for e, (t, T) in enumerate(qk_tiles(l, j)):
                        dve.wait_ge(qk_hi, t + 1)
                        hi = kH[:, e, 0:T] if j == 1 else actH[:, 2 * (j - 2) + e, 0:T]
                        lo = kL[:, e, 0:T] if j == 1 else actL[:, 2 * (j - 2) + e, 0:T]
                        nc.vector.tensor_tensor(lo, qn[:, e, 0:T], hi.bitcast(F32), ALU.subtract).then_inc(qk_ready, 1)

                for j in range(1, 8):
                    if j < 6:
                        prep(n + j + 1, (n + j + 1) % 2)
                    if 1 <= j - 2 < 6:
                        rotate(j - 2)
                    if 1 <= j - 1 < 6:
                        normed(j - 1)

            def attention(l):
                A0, sets = set0[l], SETS[l]

                def maxima(i):
                    kv, qb = sets[i]
                    k0, nkb = keys(qb)
                    dve.wait_ge(at_score, A0 + i + 1)
                    if qb < 2:
                        other = PS[:, 0:GRP, (1 - qb) * P:(2 - qb) * P]
                        nc.vector.tensor_tensor(other, other, amask[:, qb:qb + 1, :].to_broadcast([P, GRP, P]), ALU.add).then_inc(at_masked, 1)
                        dve.wait_ge(at_masked, masked(l, i) + 1)
                    nc.vector.tensor_reduce(small[:, 0:GRP], PS[:, 0:GRP, 0:nkb * P], AX.X, ALU.max).then_inc(at_max, 1)
                    dve.wait_ge(at_max, A0 + i + 1)
                    ns = negsink[:, HEADS * l + GRP * kv:HEADS * l + GRP * (kv + 1)]
                    nc.vector.scalar_tensor_tensor(small[:, 8:12], small[:, 0:GRP], -SCALE, ns, ALU.mult, ALU.min).then_inc(at_negmax, 1)
                    dve.wait_ge(at_negmax, A0 + i + 1)
                    nc.vector.tensor_tensor(small[:, 12:16], small[:, 8:12], ns, ALU.subtract).then_inc(at_nm, 1)

                def masked(l, i):
                    return sum(qb < 2 for s in SETS[:l] for _, qb in s) + sum(qb < 2 for _, qb in SETS[l][:i])

                maxima(0)
                for i, (kv, qb) in enumerate(sets):
                    k0, nkb = keys(qb)
                    dve.wait_ge(at_exp, A0 + i + 1)
                    nc.vector.tensor_tensor(small[:, 28:32], small[:, 16:20], small[:, 24:28], ALU.add).then_inc(at_den, 1)
                    dve.wait_ge(at_den, A0 + i + 1)
                    nc.vector.reciprocal(small[:, 28:32], small[:, 28:32]).then_inc(at_rden, 1)
                    dve.wait_ge(at_rden, A0 + i + 1)
                    for g in range(GRP):
                        ins = nc.vector.tensor_scalar(prob[:, g, 0:nkb * P], prob[:, g, 0:nkb * P], small[:, 28 + g:29 + g], None, ALU.mult)
                    ins.then_inc(at_prob, 1)
                    if i + 1 < len(sets):
                        maxima(i + 1)
                    dve.wait_ge(at_pth, A0 + i + 1)
                    nc.vector.tensor_tensor(ptL[:, 0:nkb, :], PS[:, 4:4 + nkb, :], ptH[:, 0:nkb, :].bitcast(F32), ALU.subtract).then_inc(at_ptl, 1)
                    dve.wait_ge(at_yh, A0 + i + 1)
                    heads, cols = slice(GRP * kv, GRP * (kv + 1)), slice(qb * P, (qb + 1) * P)
                    nc.vector.tensor_tensor(actL[:, heads, cols], PS[:, 4, :].rearrange("p (g q) -> p g q", g=GRP),
                                            actH[:, heads, cols].bitcast(F32), ALU.subtract).then_inc(at_yl, 1)

            def branch(l, which):
                T = qtokens(l)
                n = START[(("branch_a", "branch_g")[which], l)]
                c0 = 8 * l + 4 * which
                with dve.Fori(0, 4) as i:
                    prep(n + 2 * i + 1, (n + 1) % 2)
                    prep(n + 2 * i + 2, n % 2)
                    dve.wait_ge(unit_done, n + 2 * i + 2)
                    dve.wait_ge(sig_done, c0 + i + 1)
                    mv = merged[:, bass.ds(2 * i, 2), 0:T]
                    if which == 0:
                        nc.vector.tensor_tensor(mv, gate[:, :, 0:T], PS[:, 2:4, 0:T], ALU.mult).then_inc(br_done, 1)
                    else:
                        dve.wait_ge(br_done, c0 + i)
                        nc.vector.tensor_tensor(mpart[:, :, 0:T], gate[:, :, 0:T], PS[:, 2:4, 0:T], ALU.mult).then_inc(br_part, 1)
                        dve.wait_ge(br_part, 4 * l + i + 1)
                        nc.vector.tensor_tensor(mv, mv, mpart[:, :, 0:T], ALU.add).then_inc(br_done, 1)

            def gla_head(l, h, n):
                q, T = GH * l + h, qtokens(l)
                nb, c = T // P, 9 * (GH * l + h)
                pr = h % 2
                dve.wait_ge(lg_done, q + 1)
                for d, at in ((0, BIAS_F), (1, BIAS_B)):
                    nc.vector.tensor_scalar(dq[:, 0, d, :], PS[:, 6 + d, :], vecT[:, at + GH * l + h:at + GH * l + h + 1], 0.0,
                                            ALU.add, ALU.min).then_inc(lg_min, 1)
                dve.wait_ge(lg_ln, q + 1)
                nc.vector.tensor_tensor(dq[:, 0, :, :], dq[:, 0, :, :], b2[:], ALU.subtract).then_inc(g_ready, 1)
                dve.wait_ge(g_ready, q + 1)
                for b in range(NTB):
                    blk = slice(b * P, (b + 1) * P)
                    nc.vector.tensor_tensor_scan(b2[:, 0, blk], ones[:], dq[:, 0, 0, blk], 0.0, ALU.mult, ALU.add)
                    back = slice(T2 - 1 - b * P, T2 - 1 - (b + 1) * P if b < NTB - 1 else None, -1)
                    ins = nc.vector.tensor_tensor_scan(b2[:, 1, back], ones[:], dq[:, 0, 1, back], 0.0, ALU.mult, ALU.add)
                ins.then_inc(b_ready, 1)
                prep(n + 1, (n + 1) % 2)
                dve.wait_ge(lv_exp, c + 1)
                dve.wait_ge(kq_ready, 2 * (2 * l + h // 2) + 2)
                kk = gkq[:, pr, 0:1, :].to_broadcast([P, 2, T2])
                nc.vector.tensor_tensor(dq[:, 0, :, :], dq[:, 0, :, :], kk, ALU.mult).then_inc(lv_prod, 1)

                def keep(i):
                    dve.wait_ge(lv_mm, 8 * q + i + 1)
                    if 7 * q + i > 1:
                        dve.wait_ge(lv_acc, 7 * q + i - 1)
                    nc.vector.copy_predicated(A[:, 0:T].rearrange("p (b i) -> p b i", i=P),
                                              lmask[:, i - 1:i, :].to_broadcast([P, nb, P]),
                                              PS[:, 4, 0:T].rearrange("p (b i) -> p b i", i=P)).then_inc(lv_acc, 1)

                def state(which):
                    if which in (0, 3):
                        src = PS[:, 1 if which else 0, 0:DV]
                        nc.vector.tensor_copy(st[:, which, :], src).then_inc(st_step, 1)
                        return
                    d, s = divmod(which, 3)
                    blk = ((2, 3, 0), (3, 2, 1))[d][s]
                    src = PS[:, d, DV:2 * DV] if s == 1 else PS[:, 5, d * DV:(d + 1) * DV]
                    nc.vector.scalar_tensor_tensor(st[:, which, :], st[:, which - 1, :], dec[:, d, blk:blk + 1], src,
                                                   ALU.mult, ALU.add).then_inc(st_step, 1)

                for i in range(1, 8):
                    dve.wait_ge(lv_exp, c + i + 1)
                    nc.vector.tensor_tensor(dq[:, i % 2, :, 0:T], dq[:, i % 2, :, 0:T], gkq[:, pr, :, 0:T], ALU.mult).then_inc(lv_prod, 1)
                    if i == 1:
                        dve.wait_ge(diag_ready, q + 1)
                    if i == 3:
                        prep(n + 2, n % 2)
                    if i >= 2:
                        keep(i - 1)
                keep(7)
                dve.wait_ge(lv_exp, c + 9)
                qq = gkq[:, pr, 1:2, 0:T].to_broadcast([P, 2, T])
                nc.vector.tensor_tensor(dq[:, 0, :, 0:T], dq[:, 0, :, 0:T], qq, ALU.mult).then_inc(lv_prod, 1)
                dve.wait_ge(u_done, q + 1)
                for w0, w1 in ((0, 3), (1, 4), (2, 5)):
                    if w0:
                        dve.wait_ge(st_step, 6 * q + 2 * w0)
                    state(w0)
                    state(w1)
                dve.wait_ge(o_rs, q + 1)
                for b in range(nb):
                    ins = nc.vector.tensor_scalar(on[:, b // 2, b % 2 * DV:b % 2 * DV + DV], PS[:, 6 + b // 2, b % 2 * DV:b % 2 * DV + DV],
                                                  small[:, 40 + b:41 + b], None, ALU.mult)
                ins.then_inc(on_ready, 1)
                dve.wait_ge(ot_done, q + 1)
                dve.wait_ge(r_ready, q + 1)
                for e in range(2):
                    w = vecT[:, GLA_NORM + 2 * l + e:GLA_NORM + 2 * l + e + 1]
                    nc.vector.scalar_tensor_tensor(dq[:, 1, e, 0:T], PS[:, 6 + e, 0:T], w, sgr[:, e, 0:T], ALU.mult, ALU.mult).then_inc(yg_f, 1)
                for e in range(2):
                    dve.wait_ge(yg_hi, 2 * q + e + 1)
                    ins = nc.vector.tensor_tensor(actL[:, 2 * h + e, 0:T], dq[:, 1, e, 0:T], actH[:, 2 * h + e, 0:T].bitcast(F32), ALU.subtract)
                ins.then_inc(yg_ready, 1)

            def gla(l):
                n = START[("gla_proj", l)]
                prep(n + 1, (n + 1) % 2)
                u = n + 1
                for pr in range(2):
                    for z in range(2):
                        prep(u + 1, (u + 1) % 2)
                        u += 1
                    for h in (2 * pr, 2 * pr + 1):
                        gla_head(l, h, u)
                        u += 2

            def merge_split(l):
                T = qtokens(l)
                for kt in range(KT):
                    dve.wait_ge(m_hi, KT * l + kt + 1)
                    nc.vector.tensor_tensor(actL[:, kt, 0:T], merged[:, kt, 0:T], actH[:, kt, 0:T].bitcast(F32), ALU.subtract).then_inc(m_ready, 1)

            def out_proj(l):
                n = START[("out", l)]
                for j in range(4):
                    prep(n + j + 1, (n + j + 1) % 2)
                dve.wait_ge(unit_done, n + 4)
                residual(None, qtokens(l))

            for l in range(DEPTH):
                norm(3 * l, T2)
                ffn(2 * l)
                norm(3 * l + 1, T2)
                attn_proj(l)
                attention(l)
                branch(l, 0)
                gla(l)
                branch(l, 1)
                merge_split(l)
                out_proj(l)
                norm(3 * l + 2, tokens(2 * l + 1))
                ffn(2 * l + 1)
            for t in range(S // P):
                dve.wait_ge(out_t, t + 1)
                nc.vector.tensor_copy(xout[:, t, :], PS[:, 2 * t:2 * t + 2, :].rearrange("p a b -> p (a b)")).then_inc(out_ready, 1)

        @block.tensor
        def _(pe):
            mm = nc.tensor.matmul

            def mm3(o, wh, wl, ah, al, start, stop):
                mm(o, wh, ah, start=start, stop=False)
                mm(o, wh, al, start=False, stop=False)
                return mm(o, wl, ah, start=False, stop=stop)

            def weights(par):
                return (WH[:, par, :].rearrange("p (k c) -> p k c", k=KT), WL[:, par, :].rearrange("p (k c) -> p k c", k=KT))

            def unit_cols(n, par, bank, rh, rl, T, tiles=2, between=None):
                pe.wait_ge(wl_ready, n + 1)
                wh, wl = weights(par)
                for m in range(tiles):
                    for kt in range(KT):
                        ins = mm3(PS[:, bank + m, 0:T], wh[:, kt, m * P:(m + 1) * P], wl[:, kt, m * P:(m + 1) * P],
                                  rh[:, kt, 0:T], rl[:, kt, 0:T], kt == 0, kt == KT - 1)
                        if between and kt % 4 == 3 and not (m == tiles - 1 and kt == KT - 1):
                            between.pop(0)()
                ins.then_inc(unit_done, 1)

            def unit_rows(n, par, bank, between=None):
                pe.wait_ge(wl_ready, n + 1)
                wh, wl = weights(par)
                for b in range(NTB):
                    o = PS[:, bank + b // 2, b % 2 * UW:b % 2 * UW + UW]
                    for kt in range(KT):
                        ah, al = hH[:, kt, b * P:(b + 1) * P], hL[:, kt, b * P:(b + 1) * P]
                        mm(o, ah, wh[:, kt, :], start=kt == 0, stop=False)
                        mm(o, ah, wl[:, kt, :], start=False, stop=False)
                        ins = mm(o, al, wh[:, kt, :], start=False, stop=kt == KT - 1)
                    if between and b < NTB - 1:
                        between.pop(0)()
                ins.then_inc(unit_done, 1)

            def unit_mod(n, q, par):
                pe.wait_ge(wl_ready, n + 1)
                if not (isinstance(q, int) and q < 2):
                    pe.wait_ge(mod_done, q - 1)
                wh, wl = weights(par)
                for m in range(2):
                    o = PS[:, 4 + par, 4 * m:4 * m + 4]
                    for kt in range(KT):
                        mm(o, wh[:, kt, m * P:(m + 1) * P], cst[:, kt, :], start=kt == 0, stop=False)
                        ins = mm(o, wl[:, kt, m * P:(m + 1) * P], cst[:, kt, :], start=False, stop=kt == KT - 1)
                ins.then_inc(unit_done, 1)

            pe.wait_ge(ident_in, 16)
            pe.wait_ge(rows_in, 16 * 9)
            nc.tensor.transpose(PS[:, 5, 0:72], rows[0:72, 0, :], ident[0:72, 0:72])
            nc.tensor.transpose(PS[:, 5, 128:200], rows[0:72, 1, :], ident[0:72, 0:72]).then_inc(vec_t, 1)
            nc.tensor.transpose(PS[:, 6, 0:48], rows[0:48, 3, :], ident[0:48, 0:48])
            nc.tensor.transpose(PS[:, 6, 64:88], rows[64:88, 3, :], ident[64:88, 64:88]).then_inc(vec_t, 1)
            nc.tensor.transpose(PS[:, 7, 0:16], rows[0:16, 2, :], ident[0:16, 0:16]).then_inc(vec_t, 1)
            pe.wait_ge(x_in, 32)
            pe.wait_ge(vec_ready, 1)
            pe.wait_ge(cond_silu, 1)
            for kt in range(KT):
                for t in range(NTB):
                    ins = nc.tensor.transpose(PS[:, kt, t * P:(t + 1) * P], xin[:, t, kt * P:(kt + 1) * P], ident[:])
                ins.then_inc(x_t, 1)
            pe.wait_ge(cst_ready, 1)
            pe.wait_ge(x_ready, KT)
            unit_mod(0, 0, 0)
            unit_mod(1, 1, 1)
            with pe.Fori(1, MOD_FIRST // 2) as i:
                for s in range(2):
                    unit_mod(2 * i + s, 2 * i + s, s)
            pe.wait_ge(const_in, 16 * 5)

            def norm(n, T):
                for kt in range(KT):
                    pe.wait_ge(sq_done, KT * n + kt + 1)
                    ins = mm(PS[:, 0, 0:T], ones[:], sq[:, kt, 0:T], start=kt == 0, stop=kt == KT - 1)
                ins.then_inc(ss_done, 1)
                pe.wait_ge(h_ready, KT * n + KT)

            def ffn(k):
                T, g0 = tokens(k), GROUPS * k
                done = 0
                for s, (iters, fill) in enumerate(FFN_SEGMENTS[k]):
                    n, per = START[("ffn_in", k, s)], 2 + fill
                    gb = g0 + done
                    with pe.Fori(0, iters) as i:
                        u = n + per * i
                        pe.wait_ge(silu_done, gb + i)
                        unit_cols(u, n % 2, 0, hH, hL, T)
                        pe.wait_ge(gated, gb + i)
                        unit_cols(u + 1, (n + 1) % 2, 2, hH, hL, T)
                        for f in range(fill):
                            unit_mod(u + 2 + f, MODQ0[(k, s)] + fill * i + f, (n + f) % 2)
                    done += iters
                n = START[("ffn_out", k)]
                pe.wait_ge(gated, g0 + GROUPS)
                pe.wait_ge(mod_done, {0: MOD_UNITS, 1: MOD_UNITS + 22}.get(k, 2 * MOD_UNITS))

                def unit_down(u, par, first, last):
                    pe.wait_ge(wl_ready, n + u + 1)
                    pe.wait_ge(hid_lo, g0 + u + 1)
                    wh = WH[:, par, :].rearrange("p (k c) -> p k c", k=2)
                    wl = WL[:, par, :].rearrange("p (k c) -> p k c", k=2)
                    for e in range(2):
                        ah = hidH[:, bass.ds(2 * u + e, 1), 0:T].rearrange("p a t -> p (a t)")
                        al = hidL[:, bass.ds(2 * u + e, 1), 0:T].rearrange("p a t -> p (a t)")
                        for m in range(KT):
                            ins = mm3(PS[:, m, 0:T], wh[:, e, m * P:(m + 1) * P], wl[:, e, m * P:(m + 1) * P], ah, al,
                                      first and e == 0, last and e == 1)
                    ins.then_inc(unit_done, 1)

                unit_down(0, n % 2, True, False)
                with pe.Fori(0, (GROUPS - 3) // 2) as i:
                    for s in range(2):
                        unit_down(2 * i + s + 1, (n + s + 1) % 2, False, False)
                unit_down(GROUPS - 2, (n + GROUPS - 2) % 2, False, False)
                unit_down(GROUPS - 1, (n + GROUPS - 1) % 2, False, True)

            def qk_tiles(l, j):
                return [(tile0 * l + 2 * (j - 1) + e, T2 if j == 1 else qtokens(l)) for e in range(2)]

            def attn_proj(l):
                n = START[("attn_proj", l)]
                pe.wait_ge(x_ready, KT * (3 * l + 2))
                unit_rows(n, n % 2, 0)

                def sums(j):
                    for e, (t, T) in enumerate(qk_tiles(l, j)):
                        pe.wait_ge(qk_sq, t + 1)
                        if t >= 2:
                            pe.wait_ge(qk_ln, t - 1)
                        mm(PS[:, 6 + e, 0:T], ones[:], qsq[:, e, 0:T], start=True, stop=True).then_inc(qk_ss, 1)

                def swaps(j):
                    for e, (t, T) in enumerate(qk_tiles(l, j)):
                        pe.wait_ge(qk_n, t + 1)
                        mm(PS[:, 2 * (j % 3) + e, 0:S], swap[:], qn[:, e, 0:S], start=True, stop=True).then_inc(qk_swap, 1)

                for j in range(1, 8):
                    if j < 6:
                        if j == 3:
                            pe.wait_ge(v_ready, l + 1)
                        elif j > 3:
                            pe.wait_ge(qk_parts, tile0 * l + 2 * (j - 3))
                        unit_cols(n + j, (n + j) % 2, 2 * (j % 3), hH, hL, T2 if j == 1 else qtokens(l))
                    if 1 <= j - 2 < 6:
                        swaps(j - 2)
                    if 1 <= j - 1 < 6:
                        sums(j - 1)

            def attention(l):
                A0, sets = set0[l], SETS[l]

                def scores(i):
                    kv, qb = sets[i]
                    k0, nkb = keys(qb)
                    if i == 0:
                        pe.wait_ge(qk_ready, tile0 * (l + 1))
                    else:
                        pe.wait_ge(at_exp, A0 + i)
                    kc = slice(k0, k0 + nkb * P)
                    for g in range(GRP):
                        q = slice(qb * P, (qb + 1) * P)
                        ins = mm3(PS[:, g, 0:nkb * P], actH[:, GRP * kv + g, q], actL[:, GRP * kv + g, q],
                                  kH[:, kv, kc], kL[:, kv, kc], True, True)
                    ins.then_inc(at_score, 1)

                scores(0)
                for i, (kv, qb) in enumerate(sets):
                    k0, nkb = keys(qb)
                    if i + 1 < len(sets):
                        scores(i + 1)
                    pe.wait_ge(at_prob, A0 + i + 1)
                    if i:
                        pe.wait_ge(at_yl, A0 + i)
                    for b in range(nkb):
                        for g in range(GRP):
                            ins = nc.tensor.transpose(PS[:, 4 + b, g * P:(g + 1) * P], prob[:, g, b * P:(b + 1) * P], ident[:])
                    ins.then_inc(at_t, 1)
                    pe.wait_ge(at_ptl, A0 + i + 1)
                    for b in range(nkb):
                        kb = k0 // P + b
                        v = slice(kv * P, (kv + 1) * P)
                        ins = mm3(PS[:, 4, :], vH[:, kb, v], vL[:, kb, v], ptH[:, b, :], ptL[:, b, :], b == 0, b == nkb - 1)
                    ins.then_inc(at_out, 1)

            def branch(l, which):
                T = qtokens(l)
                n = START[(("branch_a", "branch_g")[which], l)]
                c0 = 8 * l + 4 * which
                if which == 0:
                    pe.wait_ge(at_yl, set0[l] + len(SETS[l]))
                else:
                    pe.wait_ge(yg_ready, GH * (l + 1))
                with pe.Fori(0, 4) as i:
                    pe.wait_ge(sig_done, c0 + i)
                    unit_cols(n + 2 * i, n % 2, 0, hH, hL, T)
                    pe.wait_ge(br_done, c0 + i)
                    unit_cols(n + 2 * i + 1, (n + 1) % 2, 2, actH, actL, T)

            def gla_head(l, h, n):
                q, T = GH * l + h, qtokens(l)
                nb, c = T // P, 9 * (GH * l + h)
                pr = h % 2

                def logits():
                    pe.wait_ge(gw_in, 32 * (l + 1))
                    if q:
                        pe.wait_ge(yg_f, 2 * q)
                    for d in range(2):
                        ins = mm(PS[:, 6 + d, :], gw[:, d, h * P:(h + 1) * P], lrT[:], start=True, stop=True)
                    ins.then_inc(lg_done, 1)

                def diagonal():
                    if q:
                        pe.wait_ge(st_step, 6 * q)
                    for b in range(nb):
                        blk = slice(b * P, (b + 1) * P)
                        ins = mm(PS[:, 5, blk], gkq[:, pr, 0, blk], gkq[:, pr, 1, blk], start=True, stop=True)
                    ins.then_inc(diag_mm, 1)

                def hats():
                    pe.wait_ge(lv_prod, c + 1)
                    for d in range(2):
                        for b in range(NTB):
                            ins = nc.tensor.transpose(PS[:, 6 + d, b * P:(b + 1) * P], dq[:, 0, d, b * P:(b + 1) * P], ident[:])
                    ins.then_inc(lv_mm, 1)

                def level(i):
                    pe.wait_ge(lv_prod, c + i + 1)
                    if i > 1:
                        pe.wait_ge(lv_acc, 7 * q + i - 1)
                    elif q:
                        pe.wait_ge(lv_acc, 7 * q)
                    for b in range(nb):
                        blk = slice(b * P, (b + 1) * P)
                        ins = mm(PS[:, 4, blk], dq[:, i % 2, 0, blk], dq[:, i % 2, 1, blk], start=True, stop=True)
                    ins.then_inc(lv_mm, 1)

                def updates():
                    pe.wait_ge(kh_ready, q + 1)
                    pe.wait_ge(v_gla, q + 1)
                    pe.wait_ge(diag_ready, q + 1)
                    for d, blocks in ((0, (2, 3, 0)), (1, (3, 2, 1))):
                        for s, b in enumerate(blocks):
                            o = PS[:, d, s * DV:(s + 1) * DV] if s < 2 else PS[:, 5, d * DV:(d + 1) * DV]
                            ins = mm(o, khn[:, d, b * P:(b + 1) * P], gvn[:, b, :], start=True, stop=True)
                    ins.then_inc(u_done, 1)

                logits()
                pe.wait_ge(kq_ready, 2 * (2 * l + h // 2) + 2)
                if q:
                    pe.wait_ge(st_step, 6 * q)
                unit_rows(n, n % 2, 0, [diagonal, hats, lambda: level(1)])
                if q:
                    pe.wait_ge(r_ready, q)
                unit_cols(n + 1, (n + 1) % 2, 2, hH, hL, T, between=[lambda: level(2), updates, lambda: level(3)])
                for i in range(4, 8):
                    level(i)
                pe.wait_ge(lv_acc, 7 * q + 7)
                pe.wait_ge(lv_prod, c + 9)
                pe.wait_ge(st_step, 6 * q + 6)
                for b in range(nb):
                    o = PS[:, 6 + b // 2, b % 2 * DV:b % 2 * DV + DV]
                    blk = slice(b * P, (b + 1) * P)
                    parts = [(A[:, blk], gvn[:, b, :])]
                    f, w = {0: (1, 5), 1: (2, 4), 2: (None, 3), 3: (0, None)}[b]
                    if f is not None:
                        parts.append((dq[:, 0, 0, blk], st[:, f, :]))
                    if w is not None:
                        parts.append((dq[:, 0, 1, blk], st[:, w, :]))
                    for z, (lhs, rhs) in enumerate(parts):
                        ins = mm(o, lhs, rhs, start=z == 0, stop=z == len(parts) - 1)
                ins.then_inc(o_done, 1)
                pe.wait_ge(on_ready, q + 1)
                for e in range(2):
                    for b in range(nb):
                        ins = nc.tensor.transpose(PS[:, 6 + e, b * P:(b + 1) * P],
                                                  on[:, b // 2, b % 2 * DV + e * P:b % 2 * DV + (e + 1) * P], ident[:])
                ins.then_inc(ot_done, 1)

            def gla(l):
                n = START[("gla_proj", l)]
                pe.wait_ge(sig_done, 8 * l + 4)
                pe.wait_ge(br_done, 8 * l + 4)
                unit_cols(n, n % 2, 0, hH, hL, T2, tiles=1)
                pe.wait_ge(lr_ready, l + 1)
                u = n + 1
                for pr in range(2):
                    for z in range(2):
                        if pr:
                            pe.wait_ge(st_step if z == 0 else r_ready, (6 if z == 0 else 1) * (GH * l + 2))
                        unit_cols(u, u % 2, 2 * z, hH, hL, T2 if z == 0 else qtokens(l))
                        u += 1
                    for h in (2 * pr, 2 * pr + 1):
                        gla_head(l, h, u)
                        u += 2

            def out_proj(l):
                T = qtokens(l)
                n = START[("out", l)]
                pe.wait_ge(m_ready, KT * (l + 1))
                for j in range(4):
                    unit_cols(n + j, (n + j) % 2, 2 * j, actH, actL, T)

            for l in range(DEPTH):
                norm(3 * l, T2)
                ffn(2 * l)
                norm(3 * l + 1, T2)
                attn_proj(l)
                attention(l)
                branch(l, 0)
                gla(l)
                branch(l, 1)
                out_proj(l)
                norm(3 * l + 2, tokens(2 * l + 1))
                ffn(2 * l + 1)
            pe.wait_ge(x_ready, KT * 7)
            for t in range(S // P):
                for kt in range(KT):
                    ins = nc.tensor.transpose(PS[:, 2 * t + kt // 4, kt % 4 * P:(kt % 4 + 1) * P], xT[:, kt, t * P:(t + 1) * P], ident[:])
                ins.then_inc(out_t, 1)


_INPUTS = ["x", "ctx", "w_mod", "b_mod", "norm_w", "ffn1_w13", "ffn1_w2", "ffn2_w13", "ffn2_w2", "w_in", "q_norm_w",
           "k_norm_w", "attn_sink", "gla_gate_w_fwd", "gla_gate_b_fwd", "gla_gate_w_bwd", "gla_gate_b_bwd", "gla_norm_w",
           "w_branch_attn", "w_branch_gla", "w_out"]


def shape_constants():
    p = np.arange(P)
    tok = np.arange(S)
    half, quarter = P // 2, P // 4
    grid_w = 64
    inv_freq = (np.float32(10000.0) ** (-np.arange(0, half, 2, dtype=np.float32) / np.float32(half))).astype(np.float32)
    pos = np.where((p < half)[:, None], (tok // grid_w)[None, :], (tok % grid_w)[None, :]).astype(np.float32)
    angle = (pos * inv_freq[p % quarter][:, None]).astype(np.float32)
    sign = np.where(p % half < quarter, -1.0, 1.0).astype(np.float32)[:, None]
    swap = np.zeros((P, P), np.float32)
    swap[p, np.where(p % half < quarter, p + quarter, p - quarter)] = 1.0
    q, k = p[:, None], p[None, :]
    amask = np.stack([np.where(k <= q, 0.0, -1e30), np.where(k >= q, 0.0, -1e30)], 1).astype(np.float32)
    lmask = np.stack([((q // (2 * m) == k // (2 * m)) & (q // m != k // m)) for m in LEVELS], 1).astype(np.float32)
    return {"c_ident": np.eye(P, dtype=np.float32), "c_ones": np.ones((P, P), np.float32), "c_swap": swap,
            "c_cos": np.cos(angle).astype(np.float32), "c_sin": (np.sin(angle) * sign).astype(np.float32),
            "c_amask": amask, "c_lmask": lmask}


def kernel(**inputs):
    import concourse.bacc as bacc
    from concourse.bass_utils import run_bass_kernel_spmd

    nc = bacc.Bacc("TRN2", target_bir_lowering=False, num_devices=1)
    arrays = {n: np.ascontiguousarray(inputs[n]) for n in _INPUTS}
    arrays["cond_rows"] = np.concatenate([np.asarray(inputs["c"]).reshape(KT, P), np.asarray(inputs["c_ctx"]).reshape(KT, P)])
    arrays.update(shape_constants())
    aps = {n: nc.dram_tensor(f"in_{n}", v.shape, mybir.dt.from_np(v.dtype), kind="ExternalInput").ap() for n, v in arrays.items()}
    out = nc.dram_tensor("out_x", (1, S, D), F32, kind="ExternalOutput").ap()
    hybrid_backbone(nc, aps, out)
    r = run_bass_kernel_spmd(nc, [{f"in_{n}": v for n, v in arrays.items()}], core_ids=[0])
    return r.results[0]["out_x"]
```

```python
from contextlib import ExitStack

import numpy as np
import concourse.bass as bass
import concourse.mybir as mybir

F32 = mybir.dt.float32
F32R = mybir.dt.float32r
U8 = mybir.dt.uint8
ALU = mybir.AluOpType
ACT = mybir.ActivationFunctionType
AX = mybir.AxisListType

P = 128
D = 1024
LN_EXP = "natural_log_exp_and_others"
KT = D // P
S = 256
T2 = 2 * S
NTB = T2 // P
DEPTH = 2
N_MOD = 9
EPS = 1e-6
D_FF = 2816
FT = D_FF // P
GROUPS = FT // 2
HEADS = 8
KVH = 2
GRP = HEADS // KVH
SCALE = P ** -0.5
GH = 4
DV = 256
RANK = 16
TEMP = 16.0
UW = 256
UN = KT * UW
COL = dict(ak=0, av=256, gk=512, gv=1024, lr=2048, aq=2080, gq=3104, gr=3616, ga=4640, gg=5664)
LEVELS = [64, 32, 16, 8, 4, 2, 1]
MOD_UNITS = N_MOD * D // UW
MOD_FIRST = 8
PAIR_AT = 2
MOD_GROUP = 4
FFN_SEGMENTS = [[(3, 4), (8, 2)], [(11, 2)], [(7, 2), (4, 0)], [(11, 0)]]


def schedule():
    start, n = {}, 0

    def take(name, count):
        nonlocal n
        start[name] = n
        n += count

    take("mod", MOD_FIRST)
    for l in range(DEPTH):
        for j in range(2):
            k = 2 * l + j
            if j == 1:
                take(("attn_proj", l), 6)
                take(("branch_a", l), 8)
                take(("gla_proj", l), 1 + 2 * (2 + 4))
                take(("branch_g", l), 8)
                take(("out", l), 4)
            for s, (iters, fill) in enumerate(FFN_SEGMENTS[k]):
                take(("ffn_in", k, s), iters * (2 + fill))
            take(("ffn_out", k), GROUPS)
    start["end"] = n
    return start


START = schedule()
N_UNITS = START["end"]


def hybrid_backbone(nc, a, out):
    ctx = ExitStack()
    with ctx:
        def sb(name, shape, dt=F32, stack=ctx):
            return stack.enter_context(nc.sbuf_tensor(name, shape, dt))

        def sem(name):
            return ctx.enter_context(nc.semaphore(name))

        PS = ctx.enter_context(nc.psum_tensor("PS", [P, 8, 512], F32))
        xT = sb("xT", [P, KT, T2])
        hH = sb("hH", [P, KT, T2], F32R)
        hL = sb("hL", [P, KT, T2], F32R)
        raw = sb("raw", [P, 2, UN])
        WH = sb("WH", [P, 2, UN], F32R)
        WL = sb("WL", [P, 2, UN], F32R)
        mod = sb("mod", [P, DEPTH * N_MOD * KT, 2])
        bmodT = sb("bmodT", [P, DEPTH * N_MOD * KT])
        nwT = sb("nwT", [P, DEPTH * 3 * KT])
        vecT = sb("vecT", [P, 24])
        Q_NORM, K_NORM, BIAS_F, BIAS_B, GLA_NORM = 0, 2, 4, 12, 20
        condT = sb("condT", [P, 2, KT])
        cst = sb("cst", [P, KT, P], F32R)
        hilo = sb("hilo", [4, 2])
        ident = sb("ident", [P, P])
        ones = sb("ones", [P, P])
        swap = sb("swap", [P, P])
        ropeC = sb("ropeC", [P, S])
        ropeS = sb("ropeS", [P, S])
        amask = sb("amask", [P, 2, P])
        lmask = sb("lmask", [P, len(LEVELS), P], U8)
        negsink = sb("negsink", [P, DEPTH * HEADS])
        epsc = sb("epsc", [P, 2])
        gw = sb("gw", [32, 2, GH * P])
        coefA = sb("coefA", [P, KT, 2])
        coefG = sb("coefG", [P, KT, 2])
        small = sb("small", [P, 44])
        mrow = sb("mrow", [P, MOD_GROUP, UW])
        rstd = mrow[:, 2:4, :].rearrange("p a c -> p (a c)")
        with ExitStack() as r:
            below_sq = sb("below_sq", [P, FT, T2], stack=r)
            sq = sb("sq", [P, KT, T2], stack=r)
        with ExitStack() as r:
            xin = sb("xin", [P, NTB, D], stack=r)
            rows = sb("rows", [P, 4, P], stack=r)
            xout = sb("xout", [P, S // P, D], stack=r)
            lmask_f = sb("lmask_f", [P, len(LEVELS), P], stack=r)
        with ExitStack() as r:
            hidH = sb("hidH", [P, FT, T2], F32R, stack=r)
            hidL = sb("hidL", [P, FT, T2], F32R, stack=r)
            sg = sb("sg", [P, 2, T2], stack=r)
        with ExitStack() as r:
            actH = sb("actH", [P, KT, T2], F32R, stack=r)
            actL = sb("actL", [P, KT, T2], F32R, stack=r)
            with ExitStack() as r2:
                kH = sb("kH", [P, KVH, T2], F32R, stack=r2)
                kL = sb("kL", [P, KVH, T2], F32R, stack=r2)
                vH = sb("vH", [P, NTB, UW], F32R, stack=r2)
                vL = sb("vL", [P, NTB, UW], F32R, stack=r2)
                prob = sb("prob", [P, GRP, T2], stack=r2)
                ptH = sb("ptH", [P, NTB, GRP * P], F32R, stack=r2)
                ptL = sb("ptL", [P, NTB, GRP * P], F32R, stack=r2)
                qsq = sb("qsq", [P, 2, T2], stack=r2)
                qrs = sb("qrs", [P, 2, T2], stack=r2)
                qn = sb("qn", [P, 2, T2], stack=r2)
                qt = sb("qt", [P, 2, 2, S], stack=r2)
            with ExitStack() as r2:
                merged = sb("merged", [P, KT, T2], stack=r2)
                with ExitStack() as r3:
                    gate = sb("gate", [P, 2, T2], stack=r3)
                    mpart = sb("mpart", [P, 2, T2], stack=r3)
                with ExitStack() as r3:
                    lrT = sb("lrT", [32, T2], stack=r3)
                    gkq = sb("gkq", [P, 2, 2, T2], stack=r3)
                    gvn = sb("gvn", [P, NTB, DV], stack=r3)
                    sgr = sb("sgr", [P, 2, T2], stack=r3)
                    b2 = sb("b2", [P, 2, T2], stack=r3)
                    dq = sb("dq", [P, 2, 2, T2], stack=r3)
                    A = sb("A", [P, T2], stack=r3)
                    khn = sb("khn", [P, 2, T2], stack=r3)
                    on = khn
                    st = sb("st", [P, 6, DV], stack=r3)
                    dec = sb("dec", [P, 2, NTB], stack=r3)

        const_in = sem("const_in")
        x_in = sem("x_in")
        rows_in = sem("rows_in")
        sink_in = sem("sink_in")
        gw_in = sem("gw_in")
        gw_zero = sem("gw_zero")
        out_in_dram = sem("out_in_dram")
        raw_in = [sem("raw_in0"), sem("raw_in1")]
        hi_ready = sem("hi_ready")
        lo_ready = sem("lo_ready")
        half_done = sem("half_done")
        y_done = sem("y_done")
        vec_t = sem("vec_t")
        vec_ready = sem("vec_ready")
        cond_silu = sem("cond_silu")
        cst_hi = sem("cst_hi")
        cst_ready = sem("cst_ready")
        x_t = sem("x_t")
        x_ready = sem("x_ready")
        eps_ready = sem("eps_ready")
        cst_zero = sem("cst_zero")
        hilo_ready = sem("hilo_ready")
        mod_row = sem("mod_row")
        mod_t = sem("mod_t")
        coefg_ready = sem("coefg_ready")
        mod_done = sem("mod_done")
        coef_ready = sem("coef_ready")
        sq_done = sem("sq_done")
        ss_done = sem("ss_done")
        ln_done = sem("ln_done")
        rstd_done = sem("rstd_done")
        xn_done = sem("xn_done")
        hf_done = sem("hf_done")
        h_hi = sem("h_hi")
        h_ready = sem("h_ready")
        silu_done = sem("silu_done")
        gated_a = sem("gated_a")
        gated_b = sem("gated_b")
        gate_in = [sem("gate_in0"), sem("gate_in1")]
        hid_hi = sem("hid_hi")
        hid_lo = sem("hid_lo")
        v_hi = sem("v_hi")
        v_ready = sem("v_ready")
        qk_sq = sem("qk_sq")
        qk_ss = sem("qk_ss")
        qk_ln = sem("qk_ln")
        qk_rs = sem("qk_rs")
        qk_n = sem("qk_n")
        qk_swap = sem("qk_swap")
        qk_parts = sem("qk_parts")
        qk_rot = sem("qk_rot")
        qk_hi = sem("qk_hi")
        qk_ready = sem("qk_ready")
        at_score = sem("at_score")
        at_masked = sem("at_masked")
        at_max = sem("at_max")
        at_negmax = sem("at_negmax")
        ident_in = sem("ident_in")
        lmask_in = sem("lmask_in")
        lmask_ready = sem("lmask_ready")
        at_nm = sem("at_nm")
        at_exp = sem("at_exp")
        at_den = sem("at_den")
        at_rden = sem("at_rden")
        at_prob = sem("at_prob")
        at_t = sem("at_t")
        at_pth = sem("at_pth")
        at_ptl = sem("at_ptl")
        at_out = sem("at_out")
        at_yh = sem("at_yh")
        at_yl = sem("at_yl")
        sig_done = sem("sig_done")
        br_part = sem("br_part")
        br_done = sem("br_done")
        m_hi = sem("m_hi")
        m_ready = sem("m_ready")
        lr_ready = sem("lr_ready")
        kq_ready = sem("kq_ready")
        v_gla = sem("v_gla")
        r_ready = sem("r_ready")
        lg_done = sem("lg_done")
        lg_abs = sem("lg_abs")
        lg_exp = sem("lg_exp")
        lg_ln = sem("lg_ln")
        lg_min = sem("lg_min")
        g_ready = sem("g_ready")
        b_ready = sem("b_ready")
        lv_diff = sem("lv_diff")
        lv_exp = sem("lv_exp")
        lv_prod = sem("lv_prod")
        lv_mm = sem("lv_mm")
        lv_acc = sem("lv_acc")
        diag_mm = sem("diag_mm")
        diag_ready = sem("diag_ready")
        kh_ready = sem("kh_ready")
        u_done = sem("u_done")
        st_step = sem("st_step")
        o_done = sem("o_done")
        o_sq = sem("o_sq")
        o_ln = sem("o_ln")
        o_rs = sem("o_rs")
        on_ready = sem("on_ready")
        ot_done = sem("ot_done")
        yg_f = sem("yg_f")
        yg_hi = sem("yg_hi")
        yg_ready = sem("yg_ready")
        out_t = sem("out_t")
        out_ready = sem("out_ready")

        wmod_d = [a["w_mod"][l].rearrange("(k p) c -> p k c", p=P) for l in range(DEPTH)]
        win_d = [a["w_in"][l].rearrange("(k p) c -> p k c", p=P) for l in range(DEPTH)]
        w13_d = [a[w][l].rearrange("(k p) c -> p k c", p=P) for l in range(DEPTH) for w in ("ffn1_w13", "ffn2_w13")]
        w2_d = [a[w][l].rearrange("(k p) c -> p k c", p=P) for l in range(DEPTH) for w in ("ffn1_w2", "ffn2_w2")]
        wba_d = [a["w_branch_attn"][l].rearrange("(k p) c -> p k c", p=P) for l in range(DEPTH)]
        wbg_d = [a["w_branch_gla"][l].rearrange("(k p) c -> p k c", p=P) for l in range(DEPTH)]
        wout_d = [a["w_out"][l].rearrange("(k p) c -> p k c", p=P) for l in range(DEPTH)]

        def half(t, par, e, rows):
            if rows:
                return t[:, par, e * UN // 2:(e + 1) * UN // 2]
            return t[:, par, :].rearrange("p (k e c) -> p e k c", k=KT, e=2)[:, e]

        def tokens(k):
            return T2 if k < 3 else S

        def ffn_norm(k):
            return 3 * (k // 2) + 2 * (k % 2)

        def qtokens(l):
            return T2 if l == 0 else S

        SETS = [[(kv, qb) for kv in range(KVH) for qb in range(qtokens(l) // P)] for l in range(DEPTH)]
        set0 = [0, len(SETS[0])]
        tile0 = 10

        def keys(qb):
            return (0, NTB) if qb < 2 else (S, 2)

        def blocks0(l, i):
            return sum(keys(qb)[1] for m in range(l) for _, qb in SETS[m]) + sum(keys(qb)[1] for _, qb in SETS[l][:i])

        GROUPS0, MODQ0, groups, q0 = {}, {}, MOD_FIRST // MOD_GROUP, MOD_FIRST
        for k in range(2 * DEPTH):
            for s, (iters, fill) in enumerate(FFN_SEGMENTS[k]):
                GROUPS0[(k, s)], MODQ0[(k, s)] = groups, q0
                groups += iters if fill else 0
                q0 += iters * fill
        GROUPS0["end"] = groups
        MODS_FOR_NORM = [GROUPS0[(0, 0)], GROUPS0[(1, 0)], GROUPS0[(1, 0)], GROUPS0[(2, 0)], groups, groups]
        MODS_FOR_GATE = [GROUPS0[(1, 0)]] + MODS_FOR_NORM[1:]

        FIRST_PAIRS = {START[("ffn_in", k, s)]: GROUPS * k + sum(it for it, _ in FFN_SEGMENTS[k][:s]) + 1
                       for k in range(2 * DEPTH) for s, (_, fill) in enumerate(FFN_SEGMENTS[k]) if fill == 0}

        block = ctx.enter_context(nc.Block())

        @block.sync
        def _(sp):
            sp.dma_start(rows[0:16, 2, :], a["cond_rows"]).then_inc(rows_in, 16)
            sp.dma_start(ident[:], a["c_ident"]).then_inc(ident_in, 16)
            sp.dma_start(rows[0:72, 0, :], a["b_mod"][0].rearrange("(r p) -> r p", p=P)).then_inc(rows_in, 16)
            sp.dma_start(rows[0:72, 1, :], a["b_mod"][1].rearrange("(r p) -> r p", p=P)).then_inc(rows_in, 16)
            sp.dma_start(rows[0:48, 3, :], a["norm_w"].rearrange("l j (r p) -> (l j r) p", p=P)).then_inc(rows_in, 16)
            for at, name in ((Q_NORM, "q_norm_w"), (K_NORM, "k_norm_w"), (BIAS_F, "gla_gate_b_fwd"),
                             (BIAS_B, "gla_gate_b_bwd"), (GLA_NORM, "gla_norm_w")):
                src = a[name].rearrange("l (r p) -> (l r) p", p=P)
                sp.dma_start(rows[64 + at:64 + at + src.shape[0], 3, :], src).then_inc(rows_in, 16)

            def load(n, slot, view, shape, pair=0):
                if pair == 0 and not (isinstance(n, int) and n < 2):
                    sp.wait_ge(lo_ready, 2 * n - 2)
                if pair == 1:
                    sp.wait_ge(lo_ready, 2 * n)
                dst = raw[:, slot, :].rearrange("p (k c) -> p k c", k=shape)
                sp.dma_start(dst, view).then_inc(raw_in[slot], 16)

            def load_pair(n, slot, f, view, at):
                sp.wait_ge(lo_ready, 2 * n - 2)
                dst = raw[:, slot, :].rearrange("p (k e c) -> p e k c", k=KT, e=2)
                sp.dma_start(dst[:, 0], view[:, :, 0:D_FF][:, :, bass.ds(at, P)]).then_inc(raw_in[slot], 16)
                sp.dma_start(dst[:, 1], view[:, :, D_FF:2 * D_FF][:, :, bass.ds(at, P)]).then_inc(gate_in[f], 16)

            load(0, 0, wmod_d[0][:, :, 0:UW], KT)
            load(1, 1, wmod_d[0][:, :, UW:2 * UW], KT)
            sp.dma_start(xin[:, 0:2, :], a["x"][0].rearrange("(t p) d -> p t d", p=P)).then_inc(x_in, 16)
            sp.dma_start(xin[:, 2:4, :], a["ctx"][0].rearrange("(t p) d -> p t d", p=P)).then_inc(x_in, 16)
            for dst, name in ((ones, "c_ones"), (swap, "c_swap"), (ropeC, "c_cos"), (ropeS, "c_sin")):
                sp.dma_start(dst[:], a[name]).then_inc(const_in, 16)
            sp.dma_start(amask[:], a["c_amask"]).then_inc(const_in, 16)
            sp.dma_start(lmask_f[:], a["c_lmask"]).then_inc(lmask_in, 16)
            sp.dma_start(negsink[:], a["attn_sink"].rearrange("l h -> (l h)").partition_broadcast(P)).then_inc(sink_in, 16)
            with sp.Fori(1, MOD_FIRST // 2) as i:
                for s in range(2):
                    load(2 * i + s, s, wmod_d[0][:, :, bass.ds(sp.snap((2 * i + s) * UW), UW)], KT)

            def load_gates(l):
                sp.wait_ge(gw_zero, 1)
                if l:
                    sp.wait_ge(lg_done, GH * l)
                sp.dma_start(gw[0:RANK, 0, :], a["gla_gate_w_fwd"][l]).then_inc(gw_in, 16)
                sp.dma_start(gw[RANK:2 * RANK, 1, :], a["gla_gate_w_bwd"][l]).then_inc(gw_in, 16)

            for k in range(4):
                l = k // 2
                if k % 2 == 1:
                    n = START[("attn_proj", l)]
                    cols = [COL["av"], COL["ak"]] + [COL["aq"] + j * UW for j in range(4)]
                    for j, c in enumerate(cols):
                        load(n + j, (n + j) % 2, win_d[l][:, :, c:c + UW], KT)
                    n = START[("branch_a", l)]
                    with sp.Fori(0, 4) as i:
                        load(n + 2 * i, n % 2, win_d[l][:, :, bass.ds(sp.snap(COL["ga"] + i * UW), UW)], KT, 1)
                        load(n + 2 * i + 1, (n + 1) % 2, wba_d[l][:, :, bass.ds(sp.snap(i * UW), UW)], KT, 2)
                    load_gates(l)
                    n = START[("gla_proj", l)]
                    cols = [COL["lr"]]
                    for pr in range(2):
                        cols += [COL["gk"] + pr * UW, COL["gq"] + pr * UW]
                        for h in (2 * pr, 2 * pr + 1):
                            cols += [COL["gv"] + h * UW, COL["gr"] + h * UW]
                    for j, c in enumerate(cols):
                        load(n + j, (n + j) % 2, win_d[l][:, :, c:c + UW], KT)
                    n = START[("branch_g", l)]
                    with sp.Fori(0, 4) as i:
                        load(n + 2 * i, n % 2, win_d[l][:, :, bass.ds(sp.snap(COL["gg"] + i * UW), UW)], KT, 1)
                        load(n + 2 * i + 1, (n + 1) % 2, wbg_d[l][:, :, bass.ds(sp.snap(i * UW), UW)], KT, 2)
                    n = START[("out", l)]
                    with sp.Fori(0, 2) as i:
                        for s in range(2):
                            load(n + 2 * i + s, (n + s) % 2, wout_d[l][:, :, bass.ds(sp.snap((2 * i + s) * UW), UW)], KT)
                g0 = 0
                for s, (iters, fill) in enumerate(FFN_SEGMENTS[k]):
                    n, per = START[("ffn_in", k, s)], 2 + fill
                    with sp.Fori(0, iters) as i:
                        m, (lm, c0) = fill // 2, divmod(MODQ0[(k, s)], MOD_UNITS)
                        for e in range(2):
                            for f in range(m):
                                at = e * (m + 1) + f
                                load(n + per * i + at, (n + at) % 2,
                                     wmod_d[lm][:, :, bass.ds(sp.snap((c0 + e * m + f + fill * i) * UW), UW)], KT)
                            at = e * (m + 1) + m
                            load_pair(n + per * i + at, (n + at) % 2, e, w13_d[k], sp.snap((2 * (i + g0) + e) * P))
                    g0 += iters
                n = START[("ffn_out", k)]
                with sp.Fori(0, GROUPS // 2) as i:
                    for s in range(2):
                        load(n + 2 * i + s, (n + s) % 2, w2_d[k][:, bass.ds(sp.snap((2 * i + s) * 2), 2), :], 2)
                load(n + GROUPS - 1, (n + GROUPS - 1) % 2, w2_d[k][:, FT - 2:FT, :], 2)

            sp.wait_ge(out_ready, 2)
            sp.dma_start(out[0].rearrange("(t p) d -> p t d", p=P), xout[:]).then_inc(out_in_dram, 16)
            sp.wait_ge(out_in_dram, 16)

        @block.gpsimd
        def _(pool):
            nc.gpsimd.memset(epsc[:, 0:1], EPS)
            nc.gpsimd.memset(epsc[:, 1:2], 1.0).then_inc(eps_ready, 1)
            nc.gpsimd.memset(gw[:], 0.0).then_inc(gw_zero, 1)
            nc.gpsimd.memset(cst[:, :, 4:P].bitcast(F32), 0.0).then_inc(cst_zero, 1)

            def norm(n, T):
                pool.wait_ge(rstd_done, n + 1)
                for kt in range(KT):
                    nc.gpsimd.tensor_tensor(sq[:, kt, 0:T], xT[:, kt, 0:T], rstd[:, 0:T], ALU.mult).then_inc(xn_done, 1)

            def diffs(l, q):
                T = qtokens(l)
                pool.wait_ge(b_ready, q + 1)
                for d, at in ((0, P - 1), (1, 0)):
                    b = b2[:, d, :].rearrange("p (n m) -> p n m", m=P)
                    ins = nc.gpsimd.tensor_tensor(
                        dq[:, 0, d, :].rearrange("p (n m) -> p n m", m=P),
                        b[:, :, at:at + 1].to_broadcast([P, NTB, P]), b, ALU.subtract)
                ins.then_inc(lv_diff, 1)
                for v, m in enumerate(LEVELS):
                    i = v + 1
                    if i >= 2:
                        pool.wait_ge(lv_mm, 8 * q + i - 1)
                    elif q:
                        pool.wait_ge(yg_ready, q)
                    nb = T // (2 * m)
                    bv = b2[:, :, 0:T].rearrange("p d (n s m) -> p d n s m", s=2, m=m)
                    ov = dq[:, i % 2, :, 0:T].rearrange("p d (n s m) -> p d n s m", s=2, m=m)
                    fm = bv[:, 0, :, 0, m - 1:m].to_broadcast([P, nb, m])
                    bm = bv[:, 1, :, 1, 0:1].to_broadcast([P, nb, m])
                    nc.gpsimd.tensor_tensor(ov[:, 0, :, 0, :], fm, bv[:, 0, :, 0, :], ALU.subtract)
                    nc.gpsimd.tensor_tensor(ov[:, 0, :, 1, :], bm, bv[:, 1, :, 1, :], ALU.subtract)
                    nc.gpsimd.tensor_tensor(ov[:, 1, :, 1, :], bv[:, 0, :, 1, :], fm, ALU.subtract)
                    nc.gpsimd.tensor_tensor(ov[:, 1, :, 0, :], bv[:, 1, :, 0, :], bm, ALU.subtract).then_inc(lv_diff, 1)

            for l in range(DEPTH):
                norm(3 * l, T2)
                norm(3 * l + 1, T2)
                for h in range(GH):
                    diffs(l, GH * l + h)
                norm(3 * l + 2, tokens(2 * l + 1))

        @block.scalar
        def _(act):
            def prep(n, par, rows=False, gate=None):
                if isinstance(n, int) and n >= N_UNITS:
                    return
                act.wait_ge(raw_in[par], (n // 2 + 1) * 16 if isinstance(n, int) else 8 * (n - par) + 16)
                if not (isinstance(n, int) and n < 2):
                    act.wait_ge(half_done, 2 * n - 2)
                if isinstance(n, int) and n in FIRST_PAIRS:
                    gate = (0, FIRST_PAIRS[n])
                if gate is not None:
                    act.wait_ge(gate_in[gate[0]], 16 * gate[1])
                for e in range(2):
                    nc.scalar.copy(half(WH, par, e, rows), half(raw, par, e, rows)).then_inc(hi_ready, 1)

            act.wait_ge(vec_t, 3)
            nc.scalar.activation(condT[:], PS[:, 7, 0:16].rearrange("p (c k) -> p c k", c=2), ACT.Silu).then_inc(cond_silu, 1)
            act.wait_ge(cond_silu, 1)
            nc.scalar.copy(cst[:, :, 0:2].rearrange("p k c -> p c k"), condT[:]).then_inc(cst_hi, 1)
            prep(0, 0, rows=True)
            act.wait_ge(eps_ready, 1)
            def ffn_start(n):
                k = 2 * (n // 3) + (n % 3) // 2
                return START[("ffn_in", k, 0)], k, FFN_SEGMENTS[k][0][1] // 2 if n % 3 != 1 else 0

            def first_mods(n):
                u, k, fill = ffn_start(n)
                for f in range(fill - 1):
                    prep(u + f + 1, (u + f + 1) % 2, rows=True)

            def first_pair(n):
                u, k, fill = ffn_start(n)
                if fill:
                    prep(u + fill, (u + fill) % 2, gate=(0, GROUPS * k + 1))

            def stats(n, T, width=D):
                nc.scalar.preload_act_table_set(LN_EXP)
                for kt in range(KT):
                    act.wait_ge(x_ready, KT * n + kt + 1)
                    nc.scalar.activation(sq[:, kt, 0:T], xT[:, kt, 0:T], ACT.Square).then_inc(sq_done, 1)
                act.wait_ge(ss_done, n + 1)
                nc.scalar.activation(rstd[:, 0:T], PS[:, 0, 0:T], ACT.Ln, bias=epsc[:, 0:1], scale=1.0 / width).then_inc(ln_done, 1)
                act.wait_ge(ln_done, n + 1)
                nc.scalar.activation(rstd[:, 0:T], rstd[:, 0:T], ACT.Exp, scale=-0.5).then_inc(rstd_done, 1)

            def norm(n, T):
                if n:
                    stats(n, T)
                first_mods(n)
                for kt in range(KT):
                    if kt == PAIR_AT:
                        first_pair(n)
                    act.wait_ge(hf_done, KT * n + kt + 1)
                    nc.scalar.copy(hH[:, kt, 0:T], sq[:, kt, 0:T]).then_inc(h_hi, 1)

            stats(0, T2)
            with act.Fori(0, MOD_FIRST // 2) as i:
                for s in range(2):
                    prep(2 * i + s + 1, (s + 1) % 2, rows=True)

            def ffn(k):
                T, g0 = tokens(k), GROUPS * k
                done = 0
                nc.scalar.preload_act_table(ACT.Silu)
                for s, (iters, fill) in enumerate(FFN_SEGMENTS[k]):
                    n, per = START[("ffn_in", k, s)], 2 + fill
                    gb = g0 + done
                    m = fill // 2
                    def first_preps(i):
                        for f in range(m):
                            prep(n + per * i + f + 1, (n + f + 1) % 2, rows=f < m - 1,
                                 gate=(0, gb + i + 1) if f == m - 1 else None)

                    def gate_and_up(i):
                        g = n + per * i + m
                        for f in range(m):
                            prep(g + f + 1, (n + m + f + 1) % 2, rows=True)
                        prep(g + m + 1, (n + 1) % 2, gate=(1, gb + i + 1))
                        act.wait_ge(half_done, 2 * (g + 1))
                        act.wait_ge(hid_lo, gb + i)
                        nc.scalar.activation(sg[:, 0, 0:T], PS[:, 0, 0:T], ACT.Silu).then_inc(silu_done, 1)
                        prep(g + m + 2, n % 2, rows=fill > 0, gate=(0, gb + i + 2) if fill == 0 and not isinstance(i, int) else None)

                    def hidden(i):
                        act.wait_ge(half_done, 2 * (n + per * (i + 1)))
                        nc.scalar.activation(sg[:, 1, 0:T], PS[:, 1, 0:T], ACT.Silu).then_inc(silu_done, 1)
                        act.wait_ge(gated_b, gb + i + 1)
                        nc.scalar.copy(hidH[:, bass.ds(2 * (i + done), 2), 0:T], sg[:, :, 0:T]).then_inc(hid_hi, 1)

                    if s:
                        first_preps(0)
                    with act.Fori(0, iters - 1) as i:
                        gate_and_up(i)
                        first_preps(i + 1)
                        hidden(i)
                    gate_and_up(iters - 1)
                    hidden(iters - 1)
                    done += iters
                n = START[("ffn_out", k)]
                with act.Fori(0, GROUPS // 2) as i:
                    for s in range(2):
                        prep(n + 2 * i + s + 1, (n + s + 1) % 2, rows=True)
                prep(n + GROUPS, (n + GROUPS) % 2, rows=k == 1)

            def qk_tiles(l, j):
                return [(tile0 * l + 2 * (j - 1) + e, T2 if j == 1 else qtokens(l)) for e in range(2)]

            def attn_proj(l):
                n = START[("attn_proj", l)]
                prep(n + 1, (n + 1) % 2)
                act.wait_ge(half_done, 2 * (n + 1))
                nc.scalar.copy(vH[:], PS[:, 0:2, :].rearrange("p a (b c) -> p (a b) c", c=UW)).then_inc(v_hi, 1)

                def squares(j):
                    act.wait_ge(half_done, 2 * (n + j + 1))
                    for e, (t, T) in enumerate(qk_tiles(l, j)):
                        if t >= 2:
                            act.wait_ge(qk_ss, t - 1)
                        nc.scalar.activation(qsq[:, e, 0:T], PS[:, 2 * (j % 3) + e, 0:T], ACT.Square).then_inc(qk_sq, 1)

                def rsq(j):
                    for e, (t, T) in enumerate(qk_tiles(l, j)):
                        act.wait_ge(qk_ss, t + 1)
                        if t >= 2:
                            act.wait_ge(qk_n, t - 1)
                        nc.scalar.activation(qrs[:, e, 0:T], PS[:, 6 + e, 0:T], ACT.Ln, bias=epsc[:, 0:1], scale=1.0 / P).then_inc(qk_ln, 1)
                    for e, (t, T) in enumerate(qk_tiles(l, j)):
                        act.wait_ge(qk_ln, t + 1)
                        nc.scalar.activation(qrs[:, e, 0:T], qrs[:, e, 0:T], ACT.Exp, scale=-0.5).then_inc(qk_rs, 1)

                def split(j):
                    for e, (t, T) in enumerate(qk_tiles(l, j)):
                        act.wait_ge(qk_rot, t + 1)
                        dst = kH[:, e, 0:T] if j == 1 else actH[:, 2 * (j - 2) + e, 0:T]
                        nc.scalar.copy(dst, qn[:, e, 0:T]).then_inc(qk_hi, 1)

                for j in range(1, 8):
                    if j < 6:
                        prep(n + j + 1, (n + j + 1) % 2)
                        squares(j)
                    if 1 <= j - 1 < 6:
                        rsq(j - 1)
                    if 1 <= j - 2 < 6:
                        split(j - 2)

            def attention(l):
                A0, sets = set0[l], SETS[l]

                def exps(i):
                    kv, qb = sets[i]
                    k0, nkb = keys(qb)
                    act.wait_ge(at_nm, A0 + i + 1)
                    if A0 + i:
                        act.wait_ge(at_t, blocks0(l, i))
                    for g in range(GRP):
                        nc.scalar.activation(prob[:, g, 0:nkb * P], PS[:, g, 0:nkb * P], ACT.Exp, bias=small[:, 8 + g:9 + g],
                                             scale=SCALE, accum_out=small[:, 16 + g:17 + g])
                    nc.scalar.activation(small[:, 24:28], small[:, 12:16], ACT.Exp).then_inc(at_exp, 1)

                exps(0)
                for i, (kv, qb) in enumerate(sets):
                    k0, nkb = keys(qb)
                    for b in range(nkb):
                        act.wait_ge(at_t, blocks0(l, i) + b + 1)
                        nc.scalar.copy(ptH[:, b, :], PS[:, 4 + b, :]).then_inc(at_pth, 1)
                    if i + 1 < len(sets):
                        exps(i + 1)
                    act.wait_ge(at_out, A0 + i + 1)
                    nc.scalar.copy(actH[:, GRP * kv:GRP * (kv + 1), qb * P:(qb + 1) * P],
                                   PS[:, 4, :].rearrange("p (g q) -> p g q", g=GRP)).then_inc(at_yh, 1)

            def branch(l, which):
                T = qtokens(l)
                n = START[(("branch_a", "branch_g")[which], l)]
                c0 = 8 * l + 4 * which
                nc.scalar.preload_act_table(ACT.Sigmoid)
                with act.Fori(0, 4) as i:
                    prep(n + 2 * i + 1, (n + 1) % 2)
                    act.wait_ge(half_done, 2 * (n + 2 * i + 1))
                    act.wait_ge(br_done, c0 + i)
                    nc.scalar.activation(gate[:, :, 0:T], PS[:, 0:2, 0:T], ACT.Sigmoid).then_inc(sig_done, 1)
                    prep(n + 2 * i + 2, n % 2)

            def decay(l, h):
                q = GH * l + h
                act.wait_ge(lg_done, q + 1)
                if q:
                    act.wait_ge(lv_exp, 9 * q)
                for d, at in ((0, BIAS_F), (1, BIAS_B)):
                    act.wait_ge(lg_min, 2 * q + d + 1)
                    nc.scalar.activation(b2[:, d, :], PS[:, 4 + d, :], ACT.Abs, bias=vecT[:, at + GH * l + h:at + GH * l + h + 1]).then_inc(lg_abs, 1)
                act.wait_ge(lg_abs, 2 * q + 2)
                nc.scalar.activation(b2[:], b2[:], ACT.Exp, scale=-1.0).then_inc(lg_exp, 1)
                act.wait_ge(lg_exp, q + 1)
                nc.scalar.activation(b2[:], b2[:], ACT.Ln, bias=epsc[:, 1:2]).then_inc(lg_ln, 1)

            def gla_head(l, h, n):
                q, T = GH * l + h, qtokens(l)
                nb, c = T // P, 9 * (GH * l + h)
                nc.scalar.preload_act_table_set(LN_EXP)
                if h == 0:
                    decay(l, h)
                prep(n + 1, (n + 1) % 2)
                act.wait_ge(b_ready, q + 1)
                bv = b2[:].rearrange("p d (n m) -> p d n m", m=P)
                if q:
                    act.wait_ge(st_step, 6 * q)
                nc.scalar.activation(dec[:, 0, :], bv[:, 0, :, P - 1], ACT.Exp, scale=1.0 / TEMP)
                nc.scalar.activation(dec[:, 1, :], bv[:, 1, :, 0], ACT.Exp, scale=1.0 / TEMP)
                act.wait_ge(lv_diff, 8 * q + 1)
                nc.scalar.activation(dq[:, 0, :, :], dq[:, 0, :, :], ACT.Exp, scale=1.0 / TEMP).then_inc(lv_exp, 1)
                act.wait_ge(diag_mm, q + 1)
                if q:
                    act.wait_ge(o_done, q)
                nc.scalar.activation(A[:, 0:T], PS[:, 5, 0:T], ACT.Copy, scale=2.0).then_inc(diag_ready, 1)
                act.wait_ge(half_done, 2 * (n + 1))
                nc.scalar.copy(gvn[:], PS[:, 0:2, :].rearrange("p a (b c) -> p (a b) c", c=DV)).then_inc(v_gla, 1)
                for i in range(1, 8):
                    act.wait_ge(lv_diff, 8 * q + i + 1)
                    nc.scalar.activation(dq[:, i % 2, :, 0:T], dq[:, i % 2, :, 0:T], ACT.Exp, scale=1.0 / TEMP).then_inc(lv_exp, 1)
                    if i == 1:
                        act.wait_ge(lv_mm, 8 * q + 1)
                        nc.scalar.copy(khn[:], PS[:, 6:8, :]).then_inc(kh_ready, 1)
                    if i == 3:
                        prep(n + 2, n % 2)
                act.wait_ge(lv_mm, 8 * q + 7)
                nc.scalar.activation(dq[:, 0, :, 0:T], b2[:, :, 0:T], ACT.Exp, scale=1.0 / TEMP).then_inc(lv_exp, 1)
                act.wait_ge(half_done, 2 * (n + 2))
                if q:
                    act.wait_ge(yg_f, 2 * q)
                nc.scalar.activation(sgr[:, :, 0:T], PS[:, 2:4, 0:T], ACT.Silu).then_inc(r_ready, 1)
                nc.scalar.preload_act_table_set(LN_EXP)
                act.wait_ge(o_done, q + 1)
                for b in range(nb):
                    nc.scalar.activation(khn[:, b // 2, b % 2 * DV:b % 2 * DV + DV], PS[:, 6 + b // 2, b % 2 * DV:b % 2 * DV + DV],
                                         ACT.Square, accum_out=small[:, 32 + b:33 + b]).then_inc(o_sq, 1)
                oq = o_sq_base(l, h) + nb
                act.wait_ge(o_sq, oq)
                nc.scalar.activation(small[:, 36:36 + nb], small[:, 32:32 + nb], ACT.Ln, bias=epsc[:, 0:1], scale=1.0 / DV).then_inc(o_ln, 1)
                act.wait_ge(o_ln, q + 1)
                nc.scalar.activation(small[:, 40:40 + nb], small[:, 36:36 + nb], ACT.Exp, scale=-0.5).then_inc(o_rs, 1)
                if h < GH - 1:
                    decay(l, h + 1)
                for e in range(2):
                    act.wait_ge(yg_f, 2 * q + e + 1)
                    nc.scalar.copy(actH[:, 2 * h + e, 0:T], dq[:, 1, e, 0:T]).then_inc(yg_hi, 1)

            def o_sq_base(l, h):
                return (GH * NTB + 2 * h) if l else NTB * h

            def gla(l):
                n = START[("gla_proj", l)]
                prep(n + 1, (n + 1) % 2)
                act.wait_ge(half_done, 2 * (n + 1))
                nc.scalar.copy(lrT[:], PS[0:32, 0, :]).then_inc(lr_ready, 1)
                u = n + 1
                for pr in range(2):
                    for z in range(2):
                        T = T2 if z == 0 else qtokens(l)
                        prep(u + 1, (u + 1) % 2)
                        act.wait_ge(half_done, 2 * (u + 1))
                        if 2 * l + pr:
                            act.wait_ge(lv_prod, 9 * (GH * l + 2 * pr))
                            act.wait_ge(diag_mm, GH * l + 2 * pr)
                        nc.scalar.activation(gkq[:, :, z, 0:T], PS[:, 2 * z:2 * z + 2, 0:T], ACT.Copy,
                                             scale=1.0 if z == 0 else SCALE).then_inc(kq_ready, 1)
                        u += 1
                    for h in (2 * pr, 2 * pr + 1):
                        gla_head(l, h, u)
                        u += 2

            def merge_split(l):
                T = qtokens(l)
                act.wait_ge(br_done, 8 * (l + 1))
                for kt in range(KT):
                    nc.scalar.copy(actH[:, kt, 0:T], merged[:, kt, 0:T]).then_inc(m_hi, 1)

            def out_proj(l):
                n = START[("out", l)]
                for j in range(4):
                    prep(n + j + 1, (n + j + 1) % 2, rows=j == 3 and l == 0)

            for l in range(DEPTH):
                norm(3 * l, T2)
                ffn(2 * l)
                norm(3 * l + 1, T2)
                attn_proj(l)
                attention(l)
                branch(l, 0)
                gla(l)
                branch(l, 1)
                merge_split(l)
                out_proj(l)
                norm(3 * l + 2, tokens(2 * l + 1))
                ffn(2 * l + 1)

        @block.vector
        def _(dve):
            def prep(n, par, rows=False):
                if isinstance(n, int) and n >= N_UNITS:
                    return
                for e in range(2):
                    dve.wait_ge(hi_ready, 2 * n + e + 1)
                    nc.vector.tensor_tensor(half(WL, par, e, rows), half(raw, par, e, rows),
                                            half(WH, par, e, rows).bitcast(F32), ALU.subtract).then_inc(lo_ready, 1)

            dve.wait_ge(vec_t, 1)
            nc.vector.tensor_copy(bmodT[:, 0:72], PS[:, 5, 0:72])
            nc.vector.tensor_copy(bmodT[:, 72:144], PS[:, 5, 128:200])
            dve.wait_ge(vec_t, 2)
            nc.vector.tensor_copy(nwT[:], PS[:, 6, 0:48])
            nc.vector.tensor_copy(vecT[:], PS[:, 6, 64:88]).then_inc(vec_ready, 1)
            nc.vector.tensor_tensor(hilo[:], ident[0:4, 0:2], ident[0:4, 2:4], ALU.add).then_inc(hilo_ready, 1)
            dve.wait_ge(cst_hi, 1)
            nc.vector.tensor_tensor(cst[:, :, 2:4].rearrange("p k c -> p c k"), condT[:],
                                    cst[:, :, 0:2].rearrange("p k c -> p c k").bitcast(F32), ALU.subtract).then_inc(cst_ready, 1)
            prep(0, 0, rows=True)
            for kt in range(KT):
                dve.wait_ge(x_t, kt + 1)
                nc.vector.tensor_copy(xT[:, kt, :], PS[:, kt, :]).then_inc(x_ready, 1)
            dve.wait_ge(sink_in, 16)
            nc.vector.tensor_scalar(negsink[:], negsink[:], -1.0, None, ALU.mult)
            dve.wait_ge(lmask_in, 16)
            nc.vector.tensor_copy(lmask[:], lmask_f[:]).then_inc(lmask_ready, 1)

            def mod_rows(n, f):
                dve.wait_ge(half_done, 2 * (n + 1))
                nc.vector.tensor_copy(mrow[0:4, f, :], PS[0:4, 4 + f, 0:UW]).then_inc(mod_row, 1)

            def mod_columns(size, q, group):
                dve.wait_ge(mod_t, group + 1)
                nc.vector.tensor_tensor(mod[:, bass.ds(2 * q, 2 * size), :],
                                        PS[:, 4, UW:UW + 4 * size].rearrange("p (m c) -> p m c", c=2),
                                        bmodT[:, bass.ds(2 * q, 2 * size)].unsqueeze(2).to_broadcast([P, 2 * size, 2]),
                                        ALU.add).then_inc(mod_done, 1)

            with dve.Fori(0, MOD_FIRST // MOD_GROUP) as i:
                for f in range(MOD_GROUP):
                    prep(MOD_GROUP * i + f + 1, (f + 1) % 2, rows=True)
                    if f == 2:
                        dve.wait_ge(xn_done, KT)
                    mod_rows(MOD_GROUP * i + f, f)
                mod_columns(MOD_GROUP, MOD_GROUP * i, i)

            def modcol(l, j):
                return mod[:, (N_MOD * l + j) * KT:(N_MOD * l + j + 1) * KT, :]

            def ffn_start(n):
                k = 2 * (n // 3) + (n % 3) // 2
                return START[("ffn_in", k, 0)], k, FFN_SEGMENTS[k][0][1] // 2 if n % 3 != 1 else 0

            def first_mods(n):
                u, k, fill = ffn_start(n)
                for f in range(fill - 1):
                    prep(u + f + 1, (u + f + 1) % 2, rows=True)

            def first_pair(n):
                u, k, fill = ffn_start(n)
                if fill:
                    prep(u + fill, (u + fill) % 2)

            def norm(n, T):
                l, j = divmod(n, 3)
                dve.wait_ge(mod_done, MODS_FOR_NORM[n])
                dve.wait_ge(x_ready, KT * (n + 1))
                nw = nwT[:, n * KT:(n + 1) * KT].unsqueeze(2).to_broadcast([P, KT, 2])
                nc.vector.scalar_tensor_tensor(coefA[:], modcol(l, 3 * j + 1), 1.0, nw, ALU.add, ALU.mult).then_inc(coef_ready, 1)
                dve.wait_ge(coef_ready, n + 1)
                shift = modcol(l, 3 * j)

                def lo(kt):
                    dve.wait_ge(h_hi, KT * n + kt + 1)
                    nc.vector.tensor_tensor(hL[:, kt, 0:T], sq[:, kt, 0:T], hH[:, kt, 0:T].bitcast(F32), ALU.subtract).then_inc(h_ready, 1)

                first_mods(n)
                for kt in range(KT):
                    if kt == PAIR_AT:
                        first_pair(n)
                    dve.wait_ge(xn_done, KT * n + kt + 1)
                    for c in range(T // S):
                        ins = nc.vector.tensor_scalar(sq[:, kt, c * S:(c + 1) * S], sq[:, kt, c * S:(c + 1) * S],
                                                      coefA[:, kt, c:c + 1], shift[:, kt, c:c + 1], ALU.mult, ALU.add)
                    ins.then_inc(hf_done, 1)
                    if kt:
                        lo(kt - 1)
                lo(KT - 1)

            def gate_coefs(n):
                l, j = divmod(n, 3)
                dve.wait_ge(mod_done, MODS_FOR_GATE[n])
                dve.wait_ge(x_ready, KT * (n + 1))
                nc.vector.tensor_scalar(coefG[:], modcol(l, 3 * j + 2), 1.0 if j == 1 else 0.5, None, ALU.mult).then_inc(coefg_ready, 1)
                dve.wait_ge(coefg_ready, n + 1)

            def residual(kt, T):
                for c in range(T // S):
                    ins = nc.vector.scalar_tensor_tensor(xT[:, kt, c * S:(c + 1) * S], PS[:, kt, c * S:(c + 1) * S],
                                                         coefG[:, kt, c:c + 1], xT[:, kt, c * S:(c + 1) * S], ALU.mult, ALU.add)
                ins.then_inc(x_ready, 1)

            def ffn(k):
                T, g0 = tokens(k), GROUPS * k
                done = 0
                for s, (iters, fill) in enumerate(FFN_SEGMENTS[k]):
                    n, per = START[("ffn_in", k, s)], 2 + fill
                    gb = g0 + done
                    m = fill // 2
                    def first_preps(i, begun=False):
                        for f in range(m):
                            u = n + per * i + f
                            if not begun:
                                prep(u + 1, (n + f + 1) % 2, rows=f < m - 1)
                            mod_rows(u, f)

                    def gate_and_up(i):
                        g = n + per * i + m
                        if m:
                            prep(g + 1, (n + m + 1) % 2, rows=True)
                        for f in range(1, m):
                            prep(g + f + 1, (n + m + f + 1) % 2, rows=True)
                            mod_rows(g + f, m + f - 1)
                        prep(g + m + 1, (n + 1) % 2)
                        if m:
                            mod_rows(g + m, 2 * m - 1)
                        dve.wait_ge(silu_done, 2 * (gb + i) + 1)
                        nc.vector.tensor_tensor(sg[:, 0, 0:T], sg[:, 0, 0:T], PS[:, 2, 0:T], ALU.mult).then_inc(gated_a, 1)
                        if fill:
                            mod_columns(fill, MODQ0[(k, s)] + fill * i, GROUPS0[(k, s)] + i)
                        prep(g + m + 2, n % 2, rows=fill > 0)

                    def hidden(i):
                        dve.wait_ge(silu_done, 2 * (gb + i) + 2)
                        nc.vector.tensor_tensor(sg[:, 1, 0:T], sg[:, 1, 0:T], PS[:, 3, 0:T], ALU.mult).then_inc(gated_b, 1)
                        dve.wait_ge(hid_hi, gb + i + 1)
                        nc.vector.tensor_tensor(hidL[:, bass.ds(2 * (i + done), 2), 0:T], sg[:, :, 0:T],
                                                hidH[:, bass.ds(2 * (i + done), 2), 0:T].bitcast(F32), ALU.subtract).then_inc(hid_lo, 1)

                    first_preps(0, s == 0)
                    with dve.Fori(0, iters - 1) as i:
                        gate_and_up(i)
                        first_preps(i + 1)
                        hidden(i)
                    gate_and_up(iters - 1)
                    hidden(iters - 1)
                    done += iters
                n = START[("ffn_out", k)]
                with dve.Fori(0, GROUPS // 2) as i:
                    for s in range(2):
                        prep(n + 2 * i + s + 1, (n + s + 1) % 2, rows=True)
                prep(n + GROUPS, (n + GROUPS) % 2, rows=k == 1)
                gate_coefs(ffn_norm(k))
                for kt in range(KT):
                    if kt < KT - 1:
                        dve.wait_ge(y_done, (KT - 1) * k + kt + 1)
                    else:
                        dve.wait_ge(half_done, 2 * (n + GROUPS))
                    residual(kt, T)

            def qk_tiles(l, j):
                return [(tile0 * l + 2 * (j - 1) + e, T2 if j == 1 else qtokens(l)) for e in range(2)]

            def attn_proj(l):
                n = START[("attn_proj", l)]
                prep(n + 1, (n + 1) % 2)
                dve.wait_ge(v_hi, l + 1)
                nc.vector.tensor_tensor(vL[:], PS[:, 0:2, :].rearrange("p a (b c) -> p (a b) c", c=UW),
                                        vH[:].bitcast(F32), ALU.subtract).then_inc(v_ready, 1)

                def normed(j):
                    for e, (t, T) in enumerate(qk_tiles(l, j)):
                        dve.wait_ge(qk_rs, t + 1)
                        if t >= 2:
                            dve.wait_ge(qk_ready, t - 1)
                        w = vecT[:, K_NORM + l:K_NORM + l + 1] if j == 1 else vecT[:, Q_NORM + l:Q_NORM + l + 1]
                        nc.vector.scalar_tensor_tensor(qn[:, e, 0:T], PS[:, 2 * (j % 3) + e, 0:T], w, qrs[:, e, 0:T],
                                                       ALU.mult, ALU.mult).then_inc(qk_n, 1)

                def rotate(j):
                    for e, (t, T) in enumerate(qk_tiles(l, j)):
                        dve.wait_ge(qk_swap, t + 1)
                        nc.vector.tensor_tensor(qt[:, e, 0, :], qn[:, e, 0:S], ropeC[:], ALU.mult)
                        nc.vector.tensor_tensor(qt[:, e, 1, :], PS[:, 2 * (j % 3) + e, 0:S], ropeS[:], ALU.mult).then_inc(qk_parts, 1)
                    for e, (t, T) in enumerate(qk_tiles(l, j)):
                        dve.wait_ge(qk_parts, t + 1)
                        nc.vector.tensor_tensor(qn[:, e, 0:S], qt[:, e, 0, :], qt[:, e, 1, :], ALU.add).then_inc(qk_rot, 1)
                    for e, (t, T) in enumerate(qk_tiles(l, j)):
                        dve.wait_ge(qk_hi, t + 1)
                        hi = kH[:, e, 0:T] if j == 1 else actH[:, 2 * (j - 2) + e, 0:T]
                        lo = kL[:, e, 0:T] if j == 1 else actL[:, 2 * (j - 2) + e, 0:T]
                        nc.vector.tensor_tensor(lo, qn[:, e, 0:T], hi.bitcast(F32), ALU.subtract).then_inc(qk_ready, 1)

                for j in range(1, 8):
                    if j < 6:
                        prep(n + j + 1, (n + j + 1) % 2)
                    if 1 <= j - 2 < 6:
                        rotate(j - 2)
                    if 1 <= j - 1 < 6:
                        normed(j - 1)

            def attention(l):
                A0, sets = set0[l], SETS[l]

                def maxima(i):
                    kv, qb = sets[i]
                    k0, nkb = keys(qb)
                    dve.wait_ge(at_score, A0 + i + 1)
                    if qb < 2:
                        other = PS[:, 0:GRP, (1 - qb) * P:(2 - qb) * P]
                        nc.vector.tensor_tensor(other, other, amask[:, qb:qb + 1, :].to_broadcast([P, GRP, P]), ALU.add).then_inc(at_masked, 1)
                        dve.wait_ge(at_masked, masked(l, i) + 1)
                    nc.vector.tensor_reduce(small[:, 0:GRP], PS[:, 0:GRP, 0:nkb * P], AX.X, ALU.max).then_inc(at_max, 1)
                    dve.wait_ge(at_max, A0 + i + 1)
                    ns = negsink[:, HEADS * l + GRP * kv:HEADS * l + GRP * (kv + 1)]
                    nc.vector.scalar_tensor_tensor(small[:, 8:12], small[:, 0:GRP], -SCALE, ns, ALU.mult, ALU.min).then_inc(at_negmax, 1)
                    dve.wait_ge(at_negmax, A0 + i + 1)
                    nc.vector.tensor_tensor(small[:, 12:16], small[:, 8:12], ns, ALU.subtract).then_inc(at_nm, 1)

                def masked(l, i):
                    return sum(qb < 2 for s in SETS[:l] for _, qb in s) + sum(qb < 2 for _, qb in SETS[l][:i])

                def scale(i):
                    kv, qb = sets[i]
                    k0, nkb = keys(qb)
                    dve.wait_ge(at_exp, A0 + i + 1)
                    nc.vector.tensor_tensor(small[:, 28:32], small[:, 16:20], small[:, 24:28], ALU.add).then_inc(at_den, 1)
                    dve.wait_ge(at_den, A0 + i + 1)
                    nc.vector.reciprocal(small[:, 28:32], small[:, 28:32]).then_inc(at_rden, 1)
                    dve.wait_ge(at_rden, A0 + i + 1)
                    for g in range(GRP):
                        ins = nc.vector.tensor_scalar(prob[:, g, 0:nkb * P], prob[:, g, 0:nkb * P], small[:, 28 + g:29 + g], None, ALU.mult)
                    ins.then_inc(at_prob, 1)

                maxima(0)
                scale(0)
                for i, (kv, qb) in enumerate(sets):
                    k0, nkb = keys(qb)
                    if i + 1 < len(sets):
                        maxima(i + 1)
                    for b in range(nkb):
                        dve.wait_ge(at_pth, blocks0(l, i) + b + 1)
                        nc.vector.tensor_tensor(ptL[:, b, :], PS[:, 4 + b, :], ptH[:, b, :].bitcast(F32), ALU.subtract).then_inc(at_ptl, 1)
                    if i + 1 < len(sets):
                        scale(i + 1)
                    dve.wait_ge(at_yh, A0 + i + 1)
                    heads, cols = slice(GRP * kv, GRP * (kv + 1)), slice(qb * P, (qb + 1) * P)
                    nc.vector.tensor_tensor(actL[:, heads, cols], PS[:, 4, :].rearrange("p (g q) -> p g q", g=GRP),
                                            actH[:, heads, cols].bitcast(F32), ALU.subtract).then_inc(at_yl, 1)

            def branch(l, which):
                T = qtokens(l)
                n = START[(("branch_a", "branch_g")[which], l)]
                c0 = 8 * l + 4 * which
                with dve.Fori(0, 4) as i:
                    prep(n + 2 * i + 1, (n + 1) % 2)
                    prep(n + 2 * i + 2, n % 2)
                    dve.wait_ge(half_done, 2 * (n + 2 * i + 2))
                    dve.wait_ge(sig_done, c0 + i + 1)
                    mv = merged[:, bass.ds(2 * i, 2), 0:T]
                    if which == 0:
                        nc.vector.tensor_tensor(mv, gate[:, :, 0:T], PS[:, 2:4, 0:T], ALU.mult).then_inc(br_done, 1)
                    else:
                        dve.wait_ge(br_done, c0 + i)
                        nc.vector.tensor_tensor(mpart[:, :, 0:T], gate[:, :, 0:T], PS[:, 2:4, 0:T], ALU.mult).then_inc(br_part, 1)
                        dve.wait_ge(br_part, 4 * l + i + 1)
                        nc.vector.tensor_tensor(mv, mv, mpart[:, :, 0:T], ALU.add).then_inc(br_done, 1)

            def decay_min(l, h):
                q = GH * l + h
                dve.wait_ge(lg_done, q + 1)
                for d, at in ((0, BIAS_F), (1, BIAS_B)):
                    nc.vector.tensor_scalar(dq[:, 0, d, :], PS[:, 4 + d, :], vecT[:, at + GH * l + h:at + GH * l + h + 1], 0.0,
                                            ALU.add, ALU.min).then_inc(lg_min, 1)

            def decay_sums(l, h):
                q = GH * l + h
                dve.wait_ge(lg_ln, q + 1)
                nc.vector.tensor_tensor(dq[:, 0, :, :], dq[:, 0, :, :], b2[:], ALU.subtract).then_inc(g_ready, 1)
                dve.wait_ge(g_ready, q + 1)
                for b in range(NTB):
                    blk = slice(b * P, (b + 1) * P)
                    nc.vector.tensor_tensor_scan(b2[:, 0, blk], ones[:], dq[:, 0, 0, blk], 0.0, ALU.mult, ALU.add)
                    back = slice(T2 - 1 - b * P, T2 - 1 - (b + 1) * P if b < NTB - 1 else None, -1)
                    ins = nc.vector.tensor_tensor_scan(b2[:, 1, back], ones[:], dq[:, 0, 1, back], 0.0, ALU.mult, ALU.add)
                ins.then_inc(b_ready, 1)

            def gla_head(l, h, n):
                q, T = GH * l + h, qtokens(l)
                nb, c = T // P, 9 * (GH * l + h)
                pr = h % 2
                if h == 0:
                    decay_min(l, h)
                    decay_sums(l, h)
                prep(n + 1, (n + 1) % 2)
                dve.wait_ge(lv_exp, c + 1)
                dve.wait_ge(kq_ready, 2 * (2 * l + h // 2) + 2)
                kk = gkq[:, pr, 0:1, :].to_broadcast([P, 2, T2])
                nc.vector.tensor_tensor(dq[:, 0, :, :], dq[:, 0, :, :], kk, ALU.mult).then_inc(lv_prod, 1)

                def keep(i):
                    dve.wait_ge(lv_mm, 8 * q + i + 1)
                    if 7 * q + i > 1:
                        dve.wait_ge(lv_acc, 7 * q + i - 1)
                    nc.vector.copy_predicated(A[:, 0:T].rearrange("p (b i) -> p b i", i=P),
                                              lmask[:, i - 1:i, :].to_broadcast([P, nb, P]),
                                              PS[:, 4, 0:T].rearrange("p (b i) -> p b i", i=P)).then_inc(lv_acc, 1)

                def state(which):
                    if which in (0, 3):
                        src = PS[:, 1 if which else 0, 0:DV]
                        nc.vector.tensor_copy(st[:, which, :], src).then_inc(st_step, 1)
                        return
                    d, s = divmod(which, 3)
                    blk = ((2, 3, 0), (3, 2, 1))[d][s]
                    src = PS[:, d, DV:2 * DV] if s == 1 else PS[:, 5, d * DV:(d + 1) * DV]
                    nc.vector.scalar_tensor_tensor(st[:, which, :], st[:, which - 1, :], dec[:, d, blk:blk + 1], src,
                                                   ALU.mult, ALU.add).then_inc(st_step, 1)

                for i in range(1, 8):
                    dve.wait_ge(lv_exp, c + i + 1)
                    nc.vector.tensor_tensor(dq[:, i % 2, :, 0:T], dq[:, i % 2, :, 0:T], gkq[:, pr, :, 0:T], ALU.mult).then_inc(lv_prod, 1)
                    if i == 1:
                        dve.wait_ge(diag_ready, q + 1)
                    if i == 3:
                        prep(n + 2, n % 2)
                    if i >= 2:
                        keep(i - 1)
                    if i >= 5:
                        dve.wait_ge(u_done, q + 1)
                        if i > 5:
                            dve.wait_ge(st_step, 6 * q + 2 * (i - 5))
                        state(i - 5)
                        state(i - 2)
                dve.wait_ge(lv_exp, c + 9)
                qq = gkq[:, pr, 1:2, 0:T].to_broadcast([P, 2, T])
                nc.vector.tensor_tensor(dq[:, 0, :, 0:T], dq[:, 0, :, 0:T], qq, ALU.mult).then_inc(lv_prod, 1)
                keep(7)
                if h < GH - 1:
                    decay_min(l, h + 1)
                dve.wait_ge(o_rs, q + 1)
                for b in range(nb):
                    ins = nc.vector.tensor_scalar(on[:, b // 2, b % 2 * DV:b % 2 * DV + DV], PS[:, 6 + b // 2, b % 2 * DV:b % 2 * DV + DV],
                                                  small[:, 40 + b:41 + b], None, ALU.mult)
                ins.then_inc(on_ready, 1)
                dve.wait_ge(ot_done, q + 1)
                dve.wait_ge(r_ready, q + 1)
                for e in range(2):
                    w = vecT[:, GLA_NORM + 2 * l + e:GLA_NORM + 2 * l + e + 1]
                    nc.vector.scalar_tensor_tensor(dq[:, 1, e, 0:T], PS[:, 6 + e, 0:T], w, sgr[:, e, 0:T], ALU.mult, ALU.mult).then_inc(yg_f, 1)
                if h < GH - 1:
                    decay_sums(l, h + 1)
                for e in range(2):
                    dve.wait_ge(yg_hi, 2 * q + e + 1)
                    ins = nc.vector.tensor_tensor(actL[:, 2 * h + e, 0:T], dq[:, 1, e, 0:T], actH[:, 2 * h + e, 0:T].bitcast(F32), ALU.subtract)
                ins.then_inc(yg_ready, 1)

            def gla(l):
                n = START[("gla_proj", l)]
                prep(n + 1, (n + 1) % 2)
                u = n + 1
                for pr in range(2):
                    for z in range(2):
                        prep(u + 1, (u + 1) % 2)
                        u += 1
                    for h in (2 * pr, 2 * pr + 1):
                        gla_head(l, h, u)
                        u += 2

            def merge_split(l):
                T = qtokens(l)
                for kt in range(KT):
                    dve.wait_ge(m_hi, KT * l + kt + 1)
                    nc.vector.tensor_tensor(actL[:, kt, 0:T], merged[:, kt, 0:T], actH[:, kt, 0:T].bitcast(F32), ALU.subtract).then_inc(m_ready, 1)

            def out_proj(l):
                n = START[("out", l)]
                gate_coefs(3 * l + 1)
                prep(n + 1, (n + 1) % 2)
                for j in range(4):
                    if j < 3:
                        prep(n + j + 2, (n + j) % 2, rows=j == 2 and l == 0)
                    for kt in (2 * j, 2 * j + 1):
                        dve.wait_ge(half_done, 2 * n + kt + 1)
                        residual(kt, qtokens(l))

            for l in range(DEPTH):
                norm(3 * l, T2)
                ffn(2 * l)
                norm(3 * l + 1, T2)
                attn_proj(l)
                attention(l)
                branch(l, 0)
                gla(l)
                branch(l, 1)
                merge_split(l)
                out_proj(l)
                norm(3 * l + 2, tokens(2 * l + 1))
                ffn(2 * l + 1)
            for t in range(S // P):
                dve.wait_ge(out_t, t + 1)
                nc.vector.tensor_copy(xout[:, t, :], PS[:, 2 * t:2 * t + 2, :].rearrange("p a b -> p (a b)")).then_inc(out_ready, 1)

        @block.tensor
        def _(pe):
            mm = nc.tensor.matmul

            def mm3(o, wh, wl, ah, al, start, stop):
                mm(o, wh, ah, start=start, stop=False)
                mm(o, wh, al, start=False, stop=False)
                return mm(o, wl, ah, start=False, stop=stop)

            def weights(par):
                return (WH[:, par, :].rearrange("p (k c) -> p k c", k=KT), WL[:, par, :].rearrange("p (k c) -> p k c", k=KT))

            def unit_cols(n, par, bank, rh, rl, T, tiles=2, step=1, between=None, h0=None, whole=False):
                wh, wl = weights(par)
                for m in range(tiles):
                    pe.wait_ge(lo_ready, 2 * n + (m if tiles == 2 and not whole else 1) + 1)
                    for kt in range(KT):
                        if h0 is not None and m == 0:
                            pe.wait_ge(h_ready, h0 + kt + 1)
                        ins = mm3(PS[:, bank + m * step, 0:T], wh[:, kt, m * P:(m + 1) * P], wl[:, kt, m * P:(m + 1) * P],
                                  rh[:, kt, 0:T], rl[:, kt, 0:T], kt == 0, kt == KT - 1)
                        if between and kt % 2 == 1 and kt < KT - 1:
                            between.pop(0)()
                    ins.then_inc(half_done, 3 - tiles)
                    if between and m == 0 and tiles == 2:
                        between.pop(0)()

            def unit_rows(n, par, bank, between=None, h0=None):
                pe.wait_ge(lo_ready, 2 * n + 2)
                wh, wl = weights(par)
                for b in range(NTB):
                    o = PS[:, bank + b // 2, b % 2 * UW:b % 2 * UW + UW]
                    for kt in range(KT):
                        if h0 is not None and b == 0:
                            pe.wait_ge(h_ready, h0 + kt + 1)
                        ah, al = hH[:, kt, b * P:(b + 1) * P], hL[:, kt, b * P:(b + 1) * P]
                        mm(o, ah, wh[:, kt, :], start=kt == 0, stop=False)
                        mm(o, ah, wl[:, kt, :], start=False, stop=False)
                        ins = mm(o, al, wh[:, kt, :], start=False, stop=kt == KT - 1)
                    if between and b < NTB - 1:
                        between.pop(0)()
                ins.then_inc(half_done, 2)
                for step in between or ():
                    step()

            def unit_mod(n, f, par):
                wh, wl = weights(par)
                for e in range(2):
                    pe.wait_ge(lo_ready, 2 * n + e + 1)
                    for kt in range(e * KT // 2, (e + 1) * KT // 2):
                        mm(PS[:, 4 + f, 0:UW], cst[:, kt, :], wh[:, kt, :], start=kt == 0, stop=False)
                        ins = mm(PS[:, 4 + f, 0:UW], cst[:, kt, :], wl[:, kt, :], start=False, stop=kt == KT - 1)
                    ins.then_inc(half_done, 1)

            def nothing():
                pass

            def mod_turn(size, q):
                pe.wait_ge(mod_row, q)
                for f in range(size):
                    for m in range(2):
                        at = UW + 4 * f + 2 * m
                        ins = mm(PS[:, 4, at:at + 2], mrow[0:4, f, m * P:(m + 1) * P], hilo[:], start=True, stop=True)
                ins.then_inc(mod_t, 1)

            pe.wait_ge(ident_in, 16)
            pe.wait_ge(rows_in, 16 * 9)
            nc.tensor.transpose(PS[:, 5, 0:72], rows[0:72, 0, :], ident[0:72, 0:72])
            nc.tensor.transpose(PS[:, 5, 128:200], rows[0:72, 1, :], ident[0:72, 0:72]).then_inc(vec_t, 1)
            nc.tensor.transpose(PS[:, 6, 0:48], rows[0:48, 3, :], ident[0:48, 0:48])
            nc.tensor.transpose(PS[:, 6, 64:88], rows[64:88, 3, :], ident[64:88, 64:88]).then_inc(vec_t, 1)
            nc.tensor.transpose(PS[:, 7, 0:16], rows[0:16, 2, :], ident[0:16, 0:16]).then_inc(vec_t, 1)
            pe.wait_ge(x_in, 32)
            pe.wait_ge(vec_ready, 1)
            pe.wait_ge(cond_silu, 1)
            for kt in range(KT):
                for t in range(NTB):
                    ins = nc.tensor.transpose(PS[:, kt, t * P:(t + 1) * P], xin[:, t, kt * P:(kt + 1) * P], ident[:])
                ins.then_inc(x_t, 1)
            def norm(n, T):
                for kt in range(KT):
                    pe.wait_ge(sq_done, KT * n + kt + 1)
                    ins = mm(PS[:, 0, 0:T], ones[:], sq[:, kt, 0:T], start=kt == 0, stop=kt == KT - 1)
                ins.then_inc(ss_done, 1)

            pe.wait_ge(const_in, 16 * 5)
            norm(0, T2)
            pe.wait_ge(cst_ready, 1)
            pe.wait_ge(x_ready, KT)
            pe.wait_ge(cst_zero, 1)
            pe.wait_ge(hilo_ready, 1)
            with pe.Fori(0, MOD_FIRST // MOD_GROUP) as i:
                pe.wait_ge(mod_done, i)
                for f in range(MOD_GROUP):
                    unit_mod(MOD_GROUP * i + f, f, f % 2)
                mod_turn(MOD_GROUP, MOD_GROUP * (i + 1))

            def ffn(k):
                T, g0 = tokens(k), GROUPS * k
                done = 0
                for s, (iters, fill) in enumerate(FFN_SEGMENTS[k]):
                    n, per = START[("ffn_in", k, s)], 2 + fill
                    gb = g0 + done
                    with pe.Fori(0, iters) as i:
                        u = n + per * i
                        m = fill // 2
                        if fill:
                            pe.wait_ge(mod_done, GROUPS0[(k, s)] + i)
                        for f in range(m):
                            unit_mod(u + f, f, (n + f) % 2)
                        pe.wait_ge(gated_a, gb + i)
                        unit_cols(u + m, (n + m) % 2, 2, hH, hL, T, step=-2, h0=KT * ffn_norm(k) if s == 0 else None, whole=fill == 0)
                        for f in range(m):
                            unit_mod(u + m + 1 + f, m + f, (n + m + 1 + f) % 2)
                        pe.wait_ge(gated_b, gb + i)
                        unit_cols(u + fill + 1, (n + 1) % 2, 3, hH, hL, T, step=-2, between=[
                            nothing, lambda: mod_turn(fill, MODQ0[(k, s)] + fill * (i + 1))] if fill else None)
                    done += iters
                n = START[("ffn_out", k)]
                pe.wait_ge(gated_b, g0 + GROUPS)
                pe.wait_ge(mod_done, GROUPS0[(k + 1, 0)] if k < 3 else GROUPS0["end"])

                def unit_down(u, par, first, last):
                    pe.wait_ge(hid_lo, g0 + u + 1)
                    wh = WH[:, par, :].rearrange("p (k c) -> p k c", k=2)
                    wl = WL[:, par, :].rearrange("p (k c) -> p k c", k=2)
                    for e in range(2):
                        pe.wait_ge(lo_ready, 2 * (n + u) + (2 if first else e + 1))
                        ah = hidH[:, bass.ds(2 * u + e, 1), 0:T].rearrange("p a t -> p (a t)")
                        al = hidL[:, bass.ds(2 * u + e, 1), 0:T].rearrange("p a t -> p (a t)")
                        for m in range(KT):
                            ins = mm3(PS[:, m, 0:T], wh[:, e, m * P:(m + 1) * P], wl[:, e, m * P:(m + 1) * P], ah, al,
                                      first and e == 0, last and e == 1)
                            if last and e == 1 and m < KT - 1:
                                ins.then_inc(y_done, 1)
                        ins.then_inc(half_done, 1)

                unit_down(0, n % 2, True, False)
                with pe.Fori(0, (GROUPS - 3) // 2) as i:
                    for s in range(2):
                        unit_down(2 * i + s + 1, (n + s + 1) % 2, False, False)
                unit_down(GROUPS - 2, (n + GROUPS - 2) % 2, False, False)
                unit_down(GROUPS - 1, (n + GROUPS - 1) % 2, False, True)

            def qk_tiles(l, j):
                return [(tile0 * l + 2 * (j - 1) + e, T2 if j == 1 else qtokens(l)) for e in range(2)]

            def scores(l, i):
                A0, (kv, qb) = set0[l], SETS[l][i]
                k0, nkb = keys(qb)
                if i == 0:
                    pe.wait_ge(qk_ready, tile0 * l + 2 + GRP)
                    pe.wait_ge(qk_parts, tile0 * l + 8)
                else:
                    pe.wait_ge(qk_ready, tile0 * (l + 1))
                    pe.wait_ge(at_exp, A0 + i)
                kc = slice(k0, k0 + nkb * P)
                for g in range(GRP):
                    q = slice(qb * P, (qb + 1) * P)
                    ins = mm3(PS[:, g, 0:nkb * P], actH[:, GRP * kv + g, q], actL[:, GRP * kv + g, q],
                              kH[:, kv, kc], kL[:, kv, kc], True, True)
                ins.then_inc(at_score, 1)

            def attn_proj(l):
                n = START[("attn_proj", l)]
                pe.wait_ge(x_ready, KT * (3 * l + 2))
                unit_rows(n, n % 2, 0, h0=KT * (3 * l + 1))

                def sums(j):
                    for e, (t, T) in enumerate(qk_tiles(l, j)):
                        pe.wait_ge(qk_sq, t + 1)
                        if t >= 2:
                            pe.wait_ge(qk_ln, t - 1)
                        mm(PS[:, 6 + e, 0:T], ones[:], qsq[:, e, 0:T], start=True, stop=True).then_inc(qk_ss, 1)

                def swaps(j):
                    for e, (t, T) in enumerate(qk_tiles(l, j)):
                        pe.wait_ge(qk_n, t + 1)
                        mm(PS[:, 2 * (j % 3) + e, 0:S], swap[:], qn[:, e, 0:S], start=True, stop=True).then_inc(qk_swap, 1)

                for j in range(1, 8):
                    if j == 7:
                        scores(l, 0)
                    if j < 6:
                        if j == 3:
                            pe.wait_ge(v_ready, l + 1)
                        elif j > 3:
                            pe.wait_ge(qk_parts, tile0 * l + 2 * (j - 3))
                        unit_cols(n + j, (n + j) % 2, 2 * (j % 3), hH, hL, T2 if j == 1 else qtokens(l))
                    if 1 <= j - 2 < 6:
                        swaps(j - 2)
                    if 1 <= j - 1 < 6:
                        sums(j - 1)

            def attention(l):
                A0, sets = set0[l], SETS[l]

                for i, (kv, qb) in enumerate(sets):
                    k0, nkb = keys(qb)
                    if i + 1 < len(sets):
                        scores(l, i + 1)
                    pe.wait_ge(at_prob, A0 + i + 1)
                    if i:
                        pe.wait_ge(at_yl, A0 + i)
                    for b in range(nkb):
                        for g in range(GRP):
                            ins = nc.tensor.transpose(PS[:, 4 + b, g * P:(g + 1) * P], prob[:, g, b * P:(b + 1) * P], ident[:])
                        ins.then_inc(at_t, 1)
                    for b in range(nkb):
                        pe.wait_ge(at_ptl, blocks0(l, i) + b + 1)
                        kb = k0 // P + b
                        v = slice(kv * P, (kv + 1) * P)
                        ins = mm3(PS[:, 4, :], vH[:, kb, v], vL[:, kb, v], ptH[:, b, :], ptL[:, b, :], b == 0, b == nkb - 1)
                    ins.then_inc(at_out, 1)

            def branch(l, which):
                T = qtokens(l)
                n = START[(("branch_a", "branch_g")[which], l)]
                c0 = 8 * l + 4 * which
                if which == 0:
                    pe.wait_ge(at_yl, set0[l] + len(SETS[l]))
                else:
                    pe.wait_ge(yg_ready, GH * (l + 1))
                with pe.Fori(0, 4) as i:
                    pe.wait_ge(sig_done, c0 + i)
                    unit_cols(n + 2 * i, n % 2, 0, hH, hL, T)
                    pe.wait_ge(br_done, c0 + i)
                    unit_cols(n + 2 * i + 1, (n + 1) % 2, 2, actH, actL, T)

            def logits(l, h):
                pe.wait_ge(gw_in, 32 * (l + 1))
                for d in range(2):
                    ins = mm(PS[:, 4 + d, :], gw[:, d, h * P:(h + 1) * P], lrT[:], start=True, stop=True)
                ins.then_inc(lg_done, 1)

            def turn(l, h):
                nb = qtokens(l) // P
                pe.wait_ge(on_ready, GH * l + h + 1)
                for e in range(2):
                    for b in range(nb):
                        ins = nc.tensor.transpose(PS[:, 6 + e, b * P:(b + 1) * P],
                                                  on[:, b // 2, b % 2 * DV + e * P:b % 2 * DV + (e + 1) * P], ident[:])
                ins.then_inc(ot_done, 1)

            def gla_head(l, h, n):
                q, T = GH * l + h, qtokens(l)
                nb, c = T // P, 9 * (GH * l + h)
                pr = h % 2

                def turn_last():
                    turn(l, h - 1)

                def diagonal():
                    pe.wait_ge(kq_ready, 2 * (2 * l + h // 2) + 2)
                    pe.wait_ge(lg_abs, 2 * q + 2)
                    if q:
                        pe.wait_ge(st_step, 6 * q)
                    for b in range(nb):
                        blk = slice(b * P, (b + 1) * P)
                        ins = mm(PS[:, 5, blk], gkq[:, pr, 0, blk], gkq[:, pr, 1, blk], start=True, stop=True)
                    ins.then_inc(diag_mm, 1)

                def hats():
                    pe.wait_ge(lv_prod, c + 1)
                    if q:
                        pe.wait_ge(yg_f, 2 * q)
                    for d in range(2):
                        for b in range(NTB):
                            ins = nc.tensor.transpose(PS[:, 6 + d, b * P:(b + 1) * P], dq[:, 0, d, b * P:(b + 1) * P], ident[:])
                    ins.then_inc(lv_mm, 1)

                def level(i):
                    pe.wait_ge(lv_prod, c + i + 1)
                    if i > 1:
                        pe.wait_ge(lv_acc, 7 * q + i - 1)
                    elif q:
                        pe.wait_ge(lv_acc, 7 * q)
                    for b in range(nb):
                        blk = slice(b * P, (b + 1) * P)
                        ins = mm(PS[:, 4, blk], dq[:, i % 2, 0, blk], dq[:, i % 2, 1, blk], start=True, stop=True)
                    ins.then_inc(lv_mm, 1)

                def updates():
                    pe.wait_ge(kh_ready, q + 1)
                    pe.wait_ge(v_gla, q + 1)
                    pe.wait_ge(diag_ready, q + 1)
                    for d, blocks in ((0, (2, 3, 0)), (1, (3, 2, 1))):
                        for s, b in enumerate(blocks):
                            o = PS[:, d, s * DV:(s + 1) * DV] if s < 2 else PS[:, 5, d * DV:(d + 1) * DV]
                            ins = mm(o, khn[:, d, b * P:(b + 1) * P], gvn[:, b, :], start=True, stop=True)
                    ins.then_inc(u_done, 1)

                if q:
                    pe.wait_ge(st_step, 6 * q)
                if h % 2:
                    unit_rows(n, n % 2, 0, [turn_last, nothing, diagonal, hats])
                else:
                    unit_rows(n, n % 2, 0, [nothing, nothing, diagonal, hats])
                if q:
                    pe.wait_ge(r_ready, q)
                lv = [lambda i=i: level(i) for i in range(1, 8)]
                unit_cols(n + 1, (n + 1) % 2, 2, hH, hL, T, between=[lv[0], lv[1], updates] + lv[2:6])
                level(7)
                pe.wait_ge(lv_acc, 7 * q + 7)
                pe.wait_ge(lv_prod, c + 9)
                pe.wait_ge(st_step, 6 * q + 6)
                for b in range(nb):
                    o = PS[:, 6 + b // 2, b % 2 * DV:b % 2 * DV + DV]
                    blk = slice(b * P, (b + 1) * P)
                    parts = [(A[:, blk], gvn[:, b, :])]
                    f, w = {0: (1, 5), 1: (2, 4), 2: (None, 3), 3: (0, None)}[b]
                    if f is not None:
                        parts.append((dq[:, 0, 0, blk], st[:, f, :]))
                    if w is not None:
                        parts.append((dq[:, 0, 1, blk], st[:, w, :]))
                    for z, (lhs, rhs) in enumerate(parts):
                        ins = mm(o, lhs, rhs, start=z == 0, stop=z == len(parts) - 1)
                ins.then_inc(o_done, 1)
                if h < GH - 1:
                    logits(l, h + 1)

            def gla(l):
                n = START[("gla_proj", l)]
                pe.wait_ge(sig_done, 8 * l + 4)
                pe.wait_ge(br_done, 8 * l + 4)
                unit_cols(n, n % 2, 0, hH, hL, T2, tiles=1)
                pe.wait_ge(lr_ready, l + 1)
                u = n + 1
                for pr in range(2):
                    for z in range(2):
                        if pr:
                            pe.wait_ge(st_step if z == 0 else r_ready, (6 if z == 0 else 1) * (GH * l + 2))
                        between = [nothing, nothing, lambda: turn(l, 2 * pr - 1)] if z == 0 and pr else None
                        if z and not pr:
                            between = [nothing, nothing, lambda: logits(l, 0)]
                        unit_cols(u, u % 2, 2 * z, hH, hL, T2 if z == 0 else qtokens(l), between=between)
                        u += 1
                    for h in (2 * pr, 2 * pr + 1):
                        gla_head(l, h, u)
                        u += 2
                turn(l, GH - 1)

            def out_proj(l):
                T = qtokens(l)
                n = START[("out", l)]
                pe.wait_ge(m_ready, KT * (l + 1))
                for j in range(4):
                    unit_cols(n + j, (n + j) % 2, 2 * j, actH, actL, T)

            for l in range(DEPTH):
                if l:
                    norm(3 * l, T2)
                ffn(2 * l)
                norm(3 * l + 1, T2)
                attn_proj(l)
                attention(l)
                branch(l, 0)
                gla(l)
                branch(l, 1)
                out_proj(l)
                norm(3 * l + 2, tokens(2 * l + 1))
                ffn(2 * l + 1)
            pe.wait_ge(x_ready, KT * 7)
            for t in range(S // P):
                for kt in range(KT):
                    ins = nc.tensor.transpose(PS[:, 2 * t + kt // 4, kt % 4 * P:(kt % 4 + 1) * P], xT[:, kt, t * P:(t + 1) * P], ident[:])
                ins.then_inc(out_t, 1)


_INPUTS = ["x", "ctx", "w_mod", "b_mod", "norm_w", "ffn1_w13", "ffn1_w2", "ffn2_w13", "ffn2_w2", "w_in", "q_norm_w",
           "k_norm_w", "attn_sink", "gla_gate_w_fwd", "gla_gate_b_fwd", "gla_gate_w_bwd", "gla_gate_b_bwd", "gla_norm_w",
           "w_branch_attn", "w_branch_gla", "w_out"]


def shape_constants():
    p = np.arange(P)
    tok = np.arange(S)
    half, quarter = P // 2, P // 4
    grid_w = 64
    inv_freq = (np.float32(10000.0) ** (-np.arange(0, half, 2, dtype=np.float32) / np.float32(half))).astype(np.float32)
    pos = np.where((p < half)[:, None], (tok // grid_w)[None, :], (tok % grid_w)[None, :]).astype(np.float32)
    angle = (pos * inv_freq[p % quarter][:, None]).astype(np.float32)
    sign = np.where(p % half < quarter, -1.0, 1.0).astype(np.float32)[:, None]
    swap = np.zeros((P, P), np.float32)
    swap[p, np.where(p % half < quarter, p + quarter, p - quarter)] = 1.0
    q, k = p[:, None], p[None, :]
    amask = np.stack([np.where(k <= q, 0.0, -1e30), np.where(k >= q, 0.0, -1e30)], 1).astype(np.float32)
    lmask = np.stack([((q // (2 * m) == k // (2 * m)) & (q // m != k // m)) for m in LEVELS], 1).astype(np.float32)
    return {"c_ident": np.eye(P, dtype=np.float32), "c_ones": np.ones((P, P), np.float32), "c_swap": swap,
            "c_cos": np.cos(angle).astype(np.float32), "c_sin": (np.sin(angle) * sign).astype(np.float32),
            "c_amask": amask, "c_lmask": lmask}


def kernel(**inputs):
    import concourse.bacc as bacc
    from concourse.bass_utils import run_bass_kernel_spmd

    nc = bacc.Bacc("TRN2", target_bir_lowering=False, num_devices=1)
    arrays = {n: np.ascontiguousarray(inputs[n]) for n in _INPUTS}
    arrays["cond_rows"] = np.concatenate([np.asarray(inputs["c"]).reshape(KT, P), np.asarray(inputs["c_ctx"]).reshape(KT, P)])
    arrays.update(shape_constants())
    aps = {n: nc.dram_tensor(f"in_{n}", v.shape, mybir.dt.from_np(v.dtype), kind="ExternalInput").ap() for n, v in arrays.items()}
    out = nc.dram_tensor("out_x", (1, S, D), F32, kind="ExternalOutput").ap()
    hybrid_backbone(nc, aps, out)
    r = run_bass_kernel_spmd(nc, [{f"in_{n}": v for n, v in arrays.items()}], core_ids=[0])
    return r.results[0]["out_x"]
```
